# Optimizing a Trainium2 kernel written in Bass

```python
import math
import jax, jax.numpy as jnp
from jax import lax
import numpy as np

D_MODEL = 2048
BATCH = 1
SEQ = 256
DEPTH = 2

HEAD_DIM = 128
N_HEADS = D_MODEL // HEAD_DIM
D_MIX = N_HEADS * HEAD_DIM
FOX_HEADS = N_HEADS // 2
NSA_HEADS = N_HEADS - FOX_HEADS
NSA_KV_HEADS = 2
NSA_GROUP = NSA_HEADS // NSA_KV_HEADS
CMP_BLOCK = 32
CMP_STRIDE = 16
SEL_BLOCK = 64
SEL_TOPK = 16
WINDOW = 512
Q_BLOCK = 128
SEL_Q_CHUNK = 16
D_FF = 5632
CONV_WIDTH = 3
ROPE_THETA = 10000.0
FORGET_BIAS_INIT = 3.0
FORCE_BONUS = 1000.0
NEG_INF = -1e30
TINY = 1e-30
EPS = 1e-6
D_IN = 3 * FOX_HEADS * HEAD_DIM + FOX_HEADS + NSA_HEADS * HEAD_DIM + 6 * NSA_KV_HEADS * HEAD_DIM + 3 * NSA_HEADS

kernel_name = "hymba_fox_nsa_convffn_adaln"

def _rmsnorm(x, g):
    xf = x.astype(jnp.float32)
    y = xf * lax.rsqrt(jnp.mean(xf * xf, axis=-1, keepdims=True) + EPS)
    return (y * g.astype(jnp.float32)).astype(x.dtype)

def _rope_tables(s):
    inv = ROPE_THETA ** (-jnp.arange(0, HEAD_DIM, 2, dtype=jnp.float32) / HEAD_DIM)
    ang = jnp.arange(s, dtype=jnp.float32)[:, None] * inv[None, :]
    return jnp.cos(ang), jnp.sin(ang)

def _rope(t, cos, sin):
    half = HEAD_DIM // 2
    tf = t.astype(jnp.float32)
    t1, t2 = tf[..., :half], tf[..., half:]
    return jnp.concatenate([t1 * cos - t2 * sin, t1 * sin + t2 * cos], axis=-1).astype(t.dtype)

def _masked_softmax(s, mask):
    s = jnp.where(mask, s, NEG_INF)
    m = jnp.max(s, axis=-1, keepdims=True)
    p = jnp.where(mask, jnp.exp(s - m), 0.0)
    return p / jnp.maximum(jnp.sum(p, axis=-1, keepdims=True), TINY)

def _heads(t, n_heads):
    b, s, _ = t.shape
    return t.reshape(b, s, n_heads, HEAD_DIM).transpose(0, 2, 1, 3)

def _fox_attention(q, k, v, logf):
    b, h, s, d = q.shape
    cum = jnp.cumsum(logf.astype(jnp.float32), axis=-1)
    scale = 1.0 / math.sqrt(d)
    kpos = jnp.arange(s)

    def block(i):
        start = i * Q_BLOCK
        qb = lax.dynamic_slice_in_dim(q, start, Q_BLOCK, axis=2)
        cb = lax.dynamic_slice_in_dim(cum, start, Q_BLOCK, axis=2)
        sc = jnp.einsum('bhqd,bhkd->bhqk', qb, k, preferred_element_type=jnp.float32) * scale \
            + cb[..., :, None] - cum[..., None, :]
        qpos = start + jnp.arange(Q_BLOCK)
        p = _masked_softmax(sc, kpos[None, :] <= qpos[:, None])
        return jnp.einsum('bhqk,bhkd->bhqd', p.astype(v.dtype), v)

    out = lax.map(block, jnp.arange(s // Q_BLOCK))
    return out.transpose(1, 2, 0, 3, 4).reshape(b, h, s, d)

def _compress(t, pos, w1, w2):
    s = t.shape[2]
    n_cmp = (s - CMP_BLOCK) // CMP_STRIDE + 1
    idx = jnp.arange(n_cmp)[:, None] * CMP_STRIDE + jnp.arange(CMP_BLOCK)[None, :]
    blk = t[:, :, idx, :] + pos
    flat = blk.reshape(blk.shape[0], blk.shape[1], n_cmp, CMP_BLOCK * HEAD_DIM)
    return jax.nn.gelu(flat @ w1) @ w2

def _gather_blocks(blocks, idx):
    return jax.vmap(jax.vmap(lambda kb, ib: kb[ib]))(blocks, idx)

def _nsa_attention(q, k_c, v_c, k_s, v_s, k_w, v_w, gates,
                   cmp_pos_k, cmp_pos_v, w_cmp1_k, w_cmp2_k, w_cmp1_v, w_cmp2_v):
    b, _, s, d = q.shape
    scale = 1.0 / math.sqrt(d)
    qg = q.reshape(b, NSA_KV_HEADS, NSA_GROUP, s, d)
    qpos_all = jnp.arange(s)

    kc = _compress(k_c, cmp_pos_k, w_cmp1_k, w_cmp2_k)
    vc = _compress(v_c, cmp_pos_v, w_cmp1_v, w_cmp2_v)
    n_cmp = kc.shape[2]
    blk_end = jnp.arange(n_cmp) * CMP_STRIDE + CMP_BLOCK - 1
    sc = jnp.einsum('bhgqd,bhnd->bhgqn', qg, kc, preferred_element_type=jnp.float32) * scale
    p_cmp = _masked_softmax(sc, blk_end[None, :] <= qpos_all[:, None])
    o_cmp = jnp.einsum('bhgqn,bhnd->bhgqd', p_cmp.astype(vc.dtype), vc)

    n_sel = s // SEL_BLOCK
    p_pad = jnp.pad(p_cmp, ((0, 0), (0, 0), (0, 0), (0, 0), (0, s // CMP_STRIDE - n_cmp)))
    imp = p_pad.reshape(b, NSA_KV_HEADS, NSA_GROUP, s, n_sel, SEL_BLOCK // CMP_STRIDE).sum(axis=(2, 5))
    cur = (qpos_all // SEL_BLOCK)[:, None]
    blk = jnp.arange(n_sel)[None, :]
    forced = (blk == 0) | (blk == cur) | (blk == cur - 1)
    score = jnp.where(blk <= cur, imp + jnp.where(forced, FORCE_BONUS, 0.0), NEG_INF)
    k_eff = min(SEL_TOPK, n_sel)
    _, sel_idx = lax.top_k(score, k_eff)

    ks_blocks = k_s.reshape(b, NSA_KV_HEADS, n_sel, SEL_BLOCK, d)
    vs_blocks = v_s.reshape(b, NSA_KV_HEADS, n_sel, SEL_BLOCK, d)

    def sel_chunk(i):
        start = i * SEL_Q_CHUNK
        qc = lax.dynamic_slice_in_dim(qg, start, SEL_Q_CHUNK, axis=3)
        ic = lax.dynamic_slice_in_dim(sel_idx, start, SEL_Q_CHUNK, axis=2)
        kg = _gather_blocks(ks_blocks, ic)
        vg = _gather_blocks(vs_blocks, ic)
        ss = jnp.einsum('bhgqd,bhqnkd->bhgqnk', qc, kg, preferred_element_type=jnp.float32) * scale
        kpos = ic[..., None] * SEL_BLOCK + jnp.arange(SEL_BLOCK)
        qpos = start + jnp.arange(SEL_Q_CHUNK)
        mask = (kpos <= qpos[:, None, None]).reshape(b, NSA_KV_HEADS, 1, SEL_Q_CHUNK, k_eff * SEL_BLOCK)
        p = _masked_softmax(ss.reshape(b, NSA_KV_HEADS, NSA_GROUP, SEL_Q_CHUNK, k_eff * SEL_BLOCK), mask)
        p = p.reshape(b, NSA_KV_HEADS, NSA_GROUP, SEL_Q_CHUNK, k_eff, SEL_BLOCK)
        return jnp.einsum('bhgqnk,bhqnkd->bhgqd', p.astype(vg.dtype), vg)

    o_sel = lax.map(sel_chunk, jnp.arange(s // SEL_Q_CHUNK))
    o_sel = o_sel.transpose(1, 2, 3, 0, 4, 5).reshape(b, NSA_KV_HEADS, NSA_GROUP, s, d)

    kw_pad = jnp.pad(k_w, ((0, 0), (0, 0), (WINDOW, 0), (0, 0)))
    vw_pad = jnp.pad(v_w, ((0, 0), (0, 0), (WINDOW, 0), (0, 0)))

    def win_block(i):
        start = i * Q_BLOCK
        qb = lax.dynamic_slice_in_dim(qg, start, Q_BLOCK, axis=3)
        kb = lax.dynamic_slice_in_dim(kw_pad, start, WINDOW + Q_BLOCK, axis=2)
        vb = lax.dynamic_slice_in_dim(vw_pad, start, WINDOW + Q_BLOCK, axis=2)
        sw = jnp.einsum('bhgqd,bhkd->bhgqk', qb, kb, preferred_element_type=jnp.float32) * scale
        kpos = start - WINDOW + jnp.arange(WINDOW + Q_BLOCK)
        qpos = start + jnp.arange(Q_BLOCK)
        mask = (kpos[None, :] <= qpos[:, None]) & (kpos[None, :] > qpos[:, None] - WINDOW) & (kpos[None, :] >= 0)
        p = _masked_softmax(sw, mask)
        return jnp.einsum('bhgqk,bhkd->bhgqd', p.astype(vb.dtype), vb)

    o_win = lax.map(win_block, jnp.arange(s // Q_BLOCK))
    o_win = o_win.transpose(1, 2, 3, 0, 4, 5).reshape(b, NSA_KV_HEADS, NSA_GROUP, s, d)

    g = gates.reshape(b, NSA_KV_HEADS, NSA_GROUP, s, 3).astype(q.dtype)
    o = g[..., 0:1] * o_cmp + g[..., 1:2] * o_sel + g[..., 2:3] * o_win
    return o.reshape(b, NSA_HEADS, s, d)

def _hybrid_mixer(h, w_in, b_fgate, cmp_pos_k, cmp_pos_v, w_cmp1_k, w_cmp2_k, w_cmp1_v, w_cmp2_v,
                  w_out, cos, sin):
    b, s, _ = h.shape
    z = h @ w_in
    sizes = [FOX_HEADS * HEAD_DIM] * 3 + [FOX_HEADS] + [NSA_HEADS * HEAD_DIM] \
        + [NSA_KV_HEADS * HEAD_DIM] * 6 + [3 * NSA_HEADS]
    (fq, fk, fv, ff, nq, kc, vc, ks, vs, kw, vw, ng) = jnp.split(z, [int(o) for o in np.cumsum(sizes)[:-1]], axis=-1)

    logf = jax.nn.log_sigmoid((ff + b_fgate).astype(jnp.float32)).transpose(0, 2, 1)
    o_fox = _fox_attention(_heads(fq, FOX_HEADS), _heads(fk, FOX_HEADS), _heads(fv, FOX_HEADS), logf)

    rq = _rope(_heads(nq, NSA_HEADS), cos, sin)
    gates = jax.nn.sigmoid(ng.astype(jnp.float32)).reshape(b, s, NSA_HEADS, 3).transpose(0, 2, 1, 3)
    o_nsa = _nsa_attention(rq,
                           _rope(_heads(kc, NSA_KV_HEADS), cos, sin), _heads(vc, NSA_KV_HEADS),
                           _rope(_heads(ks, NSA_KV_HEADS), cos, sin), _heads(vs, NSA_KV_HEADS),
                           _rope(_heads(kw, NSA_KV_HEADS), cos, sin), _heads(vw, NSA_KV_HEADS),
                           gates, cmp_pos_k, cmp_pos_v, w_cmp1_k, w_cmp2_k, w_cmp1_v, w_cmp2_v)

    o = jnp.concatenate([o_fox, o_nsa], axis=1)
    return o.transpose(0, 2, 1, 3).reshape(b, s, D_MIX) @ w_out

def _conv_ffn(h, w_up, conv_w, conv_b, w_down):
    s = h.shape[1]
    u = h @ w_up
    up = jnp.pad(u, ((0, 0), (CONV_WIDTH - 1, 0), (0, 0)))
    y = conv_b
    for j in range(CONV_WIDTH):
        y = y + conv_w[j] * up[:, j:j + s]
    gate, val = jnp.split(y, 2, axis=-1)
    return (jax.nn.silu(gate) * val) @ w_down

def setup_inputs(seed: int = 0) -> dict:
    key = jax.random.key(seed)
    ks = jax.random.split(key, 20)
    f32 = jnp.float32
    nrm = lambda k, shape, sc: jax.random.normal(k, shape, f32) * sc
    L, D, HD = DEPTH, D_MODEL, HEAD_DIM
    return {
        "x": nrm(ks[0], (BATCH, SEQ, D), 1.0),
        "c": nrm(ks[1], (BATCH, D), 1.0),
        "attn_norm_g": 1.0 + nrm(ks[2], (L, D), 0.01),
        "ffn_norm_g": 1.0 + nrm(ks[3], (L, D), 0.01),
        "w_ada": nrm(ks[4], (L, D, 6 * D), 0.5 * D ** -0.5),
        "b_ada": nrm(ks[5], (L, 6 * D), 0.01),
        "w_in": nrm(ks[6], (L, D, D_IN), D ** -0.5),
        "b_fgate": FORGET_BIAS_INIT + nrm(ks[7], (L, FOX_HEADS), 0.5),
        "cmp_pos_k": nrm(ks[8], (L, CMP_BLOCK, HD), 0.02),
        "cmp_pos_v": nrm(ks[9], (L, CMP_BLOCK, HD), 0.02),
        "w_cmp1_k": nrm(ks[10], (L, CMP_BLOCK * HD, HD), (CMP_BLOCK * HD) ** -0.5),
        "w_cmp2_k": nrm(ks[11], (L, HD, HD), HD ** -0.5),
        "w_cmp1_v": nrm(ks[12], (L, CMP_BLOCK * HD, HD), (CMP_BLOCK * HD) ** -0.5),
        "w_cmp2_v": nrm(ks[13], (L, HD, HD), HD ** -0.5),
        "w_out": nrm(ks[14], (L, D_MIX, D), D_MIX ** -0.5),
        "w_up": nrm(ks[15], (L, D, 2 * D_FF), D ** -0.5),
        "conv_w": nrm(ks[16], (L, CONV_WIDTH, 2 * D_FF), CONV_WIDTH ** -0.5),
        "conv_b": nrm(ks[17], (L, 2 * D_FF), 0.01),
        "w_down": nrm(ks[18], (L, D_FF, D), D_FF ** -0.5),
        "final_norm_g": 1.0 + nrm(ks[19], (D,), 0.01),
    }

def reference(x, c, attn_norm_g, ffn_norm_g, w_ada, b_ada, w_in, b_fgate, cmp_pos_k, cmp_pos_v,
              w_cmp1_k, w_cmp2_k, w_cmp1_v, w_cmp2_v, w_out, w_up, conv_w, conv_b, w_down,
              final_norm_g):
    s = x.shape[1]
    cos, sin = _rope_tables(s)
    c_act = jax.nn.silu(c)
    for l in range(DEPTH):
        mod = c_act @ w_ada[l] + b_ada[l]
        sh_a, sc_a, g_a, sh_f, sc_f, g_f = [m[:, None, :] for m in jnp.split(mod, 6, axis=-1)]
        h = _rmsnorm(x, attn_norm_g[l]) * (1.0 + sc_a) + sh_a
        x = x + g_a * _hybrid_mixer(h, w_in[l], b_fgate[l], cmp_pos_k[l], cmp_pos_v[l],
                                    w_cmp1_k[l], w_cmp2_k[l], w_cmp1_v[l], w_cmp2_v[l], w_out[l], cos, sin)
        h = _rmsnorm(x, ffn_norm_g[l]) * (1.0 + sc_f) + sh_f
        x = x + g_f * _conv_ffn(h, w_up[l], conv_w[l], conv_b[l], w_down[l])
    return _rmsnorm(x, final_norm_g)


_drawn_inputs = setup_inputs


def setup_inputs(seed=0):
    import zlib

    import numpy as np

    out = dict(_drawn_inputs(seed))
    spreads = {}
    factors = {'attn_norm_g': 8.0,
     'ffn_norm_g': 8.0,
     'b_ada': 3.967,
     'cmp_pos_k': 8.0,
     'cmp_pos_v': 30.48,
     'conv_b': 8.0,
     'final_norm_g': 34.213}
    for name, (base, spread) in spreads.items():
        noise = np.random.default_rng([zlib.crc32(name.encode()), seed]).standard_normal(out[name].shape)
        drawn = base * np.exp(spread * noise) if base else spread * noise
        out[name] = __import__('jax').numpy.asarray(drawn.astype(out[name].dtype))
    for name, factor in factors.items():
        out[name] = (out[name] * factor).astype(out[name].dtype)
    return out
```

```python
from contextlib import ExitStack

import numpy as np
import concourse.bass as bass
from concourse import mybir

ALU = mybir.AluOpType
ACT = mybir.ActivationFunctionType
AX = mybir.AxisListType
F32 = mybir.dt.float32
F32R = mybir.dt.float32r

P = 128
D = 2048
T = 256
TB = T // P
KT = D // P
DEPTH = 2
HD = 128
FOX = 8
NSA = 8
KV = 2
GROUP = NSA // KV
FF = 5632
FT = FF // P
D_IN = 3 * FOX * HD + FOX + NSA * HD + 6 * KV * HD + 3 * NSA
NG0 = D_IN - 3 * NSA
FF0 = 3 * FOX * HD
CB, CS = 32, 16
NC = (T - CB) // CS + 1
SCALE = 1.0 / float(np.sqrt(HD))
ROOT = float(np.sqrt(HD))
EPS = 1e-6
NEG = -1e30
TINY = 1e-30

ZQ, ZK, ZV = 0, FOX, 2 * FOX
ZNQ = 3 * FOX
ZKC, ZVC, ZKS, ZVS, ZKW, ZVW = (ZNQ + NSA + KV * n for n in range(6))
ZT = ZNQ + NSA + 6 * KV

SLOTS = 4
HSLOTS = 2
BANKS = 4
CHUNKS = 6 * D // 512

V_GA, V_GF, V_BA = 0, KT, 2 * KT
V_CW = V_BA + 6 * KT
V_CB = V_CW + 2 * FT * 3
V_BF = V_CB + 2 * FT
V_L = V_BF + FOX
V_FIN = DEPTH * V_L
V_C = V_FIN + KT
V_N = V_C + KT
M_SHA, M_SCA, M_GA, M_SHF, M_SCF, M_GF = (KT * n for n in range(6))

C_ID = 0
C_NEG = C_ID + P
C_TRI = C_NEG + P
C_COS = C_TRI + TB * T
C_SIN = C_COS + T
C_CNEG = C_SIN + T
C_C01 = C_CNEG + TB * 16
C_SEL = C_C01 + TB * 16
C_N = C_SEL + FOX


def constants():
    c = np.zeros((P, C_N), np.float32)
    p = np.arange(P)
    t = np.arange(T)
    c[:, C_ID:C_ID + P] = np.eye(P)
    c[:, C_NEG:C_NEG + P] = np.where(p[None, :] <= p[:, None], 0.0, NEG)
    for b in range(TB):
        c[:, C_TRI + b * T:C_TRI + (b + 1) * T] = t[None, :] >= b * P + p[:, None]
        seen = np.arange(NC)[None, :] * CS + CB - 1 <= (b * P + p)[:, None]
        c[:, C_CNEG + b * 16:C_CNEG + b * 16 + NC] = np.where(seen, 0.0, NEG)
        c[:, C_C01 + b * 16:C_C01 + b * 16 + NC] = seen
    half = HD // 2
    inv = np.float32(10000.0) ** (-np.arange(0, HD, 2, dtype=np.float32) / np.float32(HD))
    ang = (t.astype(np.float32)[:, None] * inv[None, :]).astype(np.float32).T
    c[:, C_COS:C_COS + T] = np.concatenate([np.cos(ang), np.cos(ang)])
    c[:half, C_SIN:C_SIN + T] = np.sin(ang)
    c[half:, C_SIN:C_SIN + T] = -np.sin(ang)
    for h in range(FOX):
        c[h, C_SEL + h] = 1.0
        c[32 + h, C_SEL + h] = 1.0
    return c


class Phase:

    def __init__(self, name, layer, iters, items, groups=0, ktiles=(), src=None, first_chunk=0):
        self.name, self.layer, self.iters, self.items = name, layer, iters, items
        self.groups, self.ktiles, self.src, self.first_chunk = groups, ktiles, src, first_chunk
        self.m_per = sum(x[0] == "M" for x in items)
        self.a_per = sum(x[0] == "A" for x in items)
        self.chunks = self.a_per // 4


def weave(groups, steps, adas, every):
    out, a = [], 0
    for g in range(groups):
        for q in range(steps):
            out.append(("M", g, q))
            if (g * steps + q + 1) % every == 0 and a < adas:
                out.append(("A", a // 4, a % 4))
                a += 1
    return out


def plan():
    four = (4, 4, 4, 4)
    down = (4,) * 8 + (3,) * 4
    only = [("A", 0, r) for r in range(4)]
    w1 = [("W", 0, r) for r in range(4)]
    ph, chunk = [], 0

    def add(name, layer, iters, items, **k):
        nonlocal chunk
        x = Phase(name, layer, iters, items, first_chunk=chunk, **k)
        chunk += x.chunks * iters
        ph.append(x)

    for l in range(DEPTH):
        a = 4 if l == 0 else 0
        if l == 0:
            add("pre", l, 8, only)
        add("fox", l, 6, weave(1, 4, a, 1), groups=1, ktiles=four)
        add("nsa", l, 5, weave(1, 4, a, 1), groups=1, ktiles=four)
        add("ext", l, 1, only)
        add("cmp", l, 1, w1)
        add("out", l, 4, weave(1, 4, a, 1), groups=1, ktiles=four)
        add("up", l, 11, weave(2, 4, a, 2), groups=2, ktiles=four)
        add("down", l, 4, weave(1, 12, 3 * a, 1), groups=1, ktiles=down)
    assert chunk == DEPTH * CHUNKS
    s = m = a = g = w = 0
    kinds = []
    for x in ph:
        x.s0, x.m0, x.a0, x.g0, x.w0 = s, m, a, g, w
        assert s % SLOTS == 0 and len(x.items) % SLOTS == 0 and m % HSLOTS == 0 and x.m_per % HSLOTS == 0
        kinds += [y[0] for y in x.items] * x.iters
        s += len(x.items) * x.iters
        m += x.m_per * x.iters
        a += x.a_per * x.iters
        g += x.groups * x.iters
        w += sum(y[0] == "W" for y in x.items) * x.iters
    return ph, kinds


def repeat(eng, start, end, body):
    if end - start == 1:
        body(start)
    elif end > start:
        with eng.Fori(start, end) as i:
            body(i)


class Chain:

    def __init__(self, eng, sem):
        self.eng, self.sem, self.base, self.k, self.i, self.per = eng, sem, 0, 0, None, 0

    def __call__(self, ins):
        ins.then_inc(self.sem, 1)
        self.k += 1
        at = self.base + self.k if self.i is None else self.i * self.per + (self.base + self.k)
        self.eng.wait_ge(self.sem, at)

    def loop(self, start, end, per, body):
        self.base, self.k = self.base + self.k, 0

        def one(i):
            self.i, self.per, self.k = i, per, 0
            self.base -= start * per
            body(i)
            self.base += start * per
            assert self.k == per, (self.k, per)

        repeat(self.eng, start, end, one)
        self.i, self.k = None, 0
        self.base += per * (end - start)


def trunk(nc, xT, par, pos, consts, w_ada, w_in, w_cmp1_k, w_cmp1_v, w_cmp2_k, w_cmp2_v,
          w_out, w_up, w_down, out):
    phases, kinds = plan()
    nm = [0]
    na = [0]
    nw = [0]
    for k in kinds:
        nm.append(nm[-1] + (k == "M"))
        na.append(na[-1] + (k == "A"))
        nw.append(nw[-1] + (k == "W"))

    def phase(name, l):
        return next(x for x in phases if x.name == name and x.layer == l)

    with ExitStack() as ctx:
        at = [(nc.sbuf_base + 31) // 32 * 32]

        def place(name, shape, dt=F32, offset=None):
            size = int(np.prod(shape[1:])) * 4
            if offset is None:
                offset = at[0]
                at[0] += (size + 31) // 32 * 32
            return nc.alloc_sbuf_tensor_at(name, shape, dt, offset=offset)

        def end_of(offset, shape):
            return offset + (int(np.prod(shape[1:])) * 4 + 31) // 32 * 32

        x_sb = place("x_sb", [P, KT, T])
        hb = place("hb", [P, KT, 2 * T], F32R)
        whi = place("whi", [P, HSLOTS, 4, 512], F32R)
        ring = at[0]
        raw = place("raw", [P, SLOTS, 4, 512])
        wlo = place("wlo", [P, SLOTS, 4, 512], F32R, offset=ring)
        par_sb = place("par_sb", [P, V_N])
        mod = place("mod", [P, DEPTH, 6 * KT])
        ones = place("ones", [P, P])
        acc = place("acc", [P, 512])
        cact = place("cact", [P, KT])
        acol = place("acol", [P, KT])
        evb = place("evb", [P, BANKS, T])
        scratch = at[0]
        ub = place("ub", [P, 4, T + 2])
        yb = place("yb", [P, 4, T])
        sb_ = place("sb_", [P, 2, T])
        scratch_end = at[0]
        c_sb = place("c_sb", [P, C_N], offset=scratch)
        o = end_of(scratch, [P, C_N])
        wx = place("wx", [P, KT, 32], offset=o)
        wxlo = place("wxlo", [P, KT, 32], F32R, offset=o)
        o = end_of(o, [P, KT, 32])
        wxhi = place("wxhi", [P, KT, 32], F32R, offset=o)
        assert end_of(o, [P, KT, 32]) <= scratch_end
        arena = at[0]
        actb = place("actb", [P, FT, 2 * T], F32R)
        arena_end = at[0]
        assert arena_end <= nc.sbuf_usable_end, (arena_end, nc.sbuf_usable_end)
        cur = [arena]

        def inside(name, shape, dt=F32):
            t = place(name, shape, dt, offset=cur[0])
            cur[0] = end_of(cur[0], shape)
            assert cur[0] <= arena_end, name
            return t

        z = inside("z", [P, ZT, T])
        nrm = place("nrm", [P, KT, T], offset=arena)
        ssum = inside("ssum", [P, T])
        rstd = inside("rstd", [P, T])
        w2 = inside("w2", [P, 2, P])
        pos_sb = inside("pos_sb", [P, 2, CB])
        lg = inside("lg", [P, TB, 32])
        eg = inside("eg", [P, TB, 32])
        gate = inside("gate", [P, TB, 3 * NSA])
        lf = inside("lf", [P, TB, FOX])
        ln1 = inside("ln1", [P, TB, FOX])
        gel = inside("gel", [P, KV * NC])
        kcT = inside("kcT", [P, KV * NC])
        vc = inside("vc", [P, KV, P])
        vsw = inside("vsw", [P, 2, KV, TB, P])
        Lb = inside("Lb", [P, T])
        Rall = inside("Rall", [P, T])
        Rb = inside("Rb", [P, T])
        before = cur[0]
        xb = inside("xb", [P, 2, CB, KV * NC])
        rtmp = inside("rtmp", [P, NSA, T])
        cur[0] = before
        qf = inside("qf", [P, T])
        qn = inside("qn", [P, T])
        vfT = inside("vfT", [P, T])
        vf = inside("vf", [P, TB, P])
        pr = inside("pr", [P, 3, 3 * P])
        prc = inside("prc", [P, TB, P])
        pt = inside("pt", [P, 3, 3 * P])
        ptc = inside("ptc", [P, TB * P])
        sc = inside("sc", [P, TB, 16])
        mx = inside("mx", [P, 4, TB])
        nb = inside("nb", [P, 4, TB])
        rs = inside("rs", [P, 4, TB])
        rr = inside("rr", [P, 4, TB])

        ps = ctx.enter_context(nc.psum_tensor("ps", [P, 8, 512], F32))

        sem = {}

        def S(name):
            if name not in sem:
                sem[name] = ctx.enter_context(nc.semaphore(name))
            return sem[name]

        full = [S(f"slot_full{n}") for n in range(SLOTS)]
        x_loaded, par_loaded, ext_loaded = S("x_loaded"), S("par_loaded"), S("ext_loaded")
        stored = S("stored")
        w_used, w1_used, ada_used = S("w_used"), S("w1_used"), S("ada_used")
        hi_ready, lo_ready = S("hi_ready"), S("lo_ready")
        ada_sum, mod_ready = S("ada_sum"), S("mod_ready")
        bank_full, half_out, bank_free = S("bank_full"), S("half_out"), S("bank_free")
        conv_y, conv_done, silu_done, prod_done, acthi, act_ready = (
            S(n) for n in ("conv_y", "conv_done", "silu_done", "prod_done", "acthi", "act_ready"))
        sq_ready, ss_ready, ssb_ready, var_ready, root_ready, t_ready, hh_ready, h_ready = (
            S(n) for n in ("sq_ready", "ss_ready", "ssb_ready", "var_ready", "root_ready", "t_ready",
                           "hh_ready", "h_ready"))
        hhi_ready = S("hhi_ready")
        x_done, cact_ready, ones_ready = S("x_done"), S("cact_ready"), S("ones_ready")
        dve_own, act_own, pool_own = S("dve_own"), S("act_own"), S("pool_own")
        xhi_ready, xlo_ready, ext_sum, lg_ready, eg_ready, lf_ready, cum_ready, bias_ready = (
            S(n) for n in ("xhi_ready", "xlo_ready", "ext_sum", "lg_ready", "eg_ready", "lf_ready",
                           "cum_ready", "bias_ready"))
        xb_ready, gel_ready, cmp_ready, cmpc_ready, vsw_t, vsw_ready = (
            S(n) for n in ("xb_ready", "gel_ready", "cmp_ready", "cmpc_ready",
                           "vsw_t", "vsw_ready"))
        zero_ready, stage_ready, r_ready, s_ready, vt_ready, vf_ready, nb_ready, p_ready, pn_ready = (
            S(n) for n in ("zero_ready", "stage_ready", "r_ready", "s_ready", "vt_ready", "vf_ready",
                           "nb_ready", "p_ready", "pn_ready"))
        pt_ready, ptc_ready, pv_ready, ohi_ready, o_done = (
            S(n) for n in ("pt_ready", "ptc_ready", "pv_ready", "ohi_ready", "o_done"))

        def modc(l, tile):
            return mod[:, l, tile:tile + 1]

        def flat(tile):
            return tile.rearrange("p o t -> p (o t)")

        def rows(w, k0, kn):
            return w[k0 * P:(k0 + kn) * P, :].rearrange("(k p) n -> p k n", p=P)

        def tiles_out(x, i=None):
            n = x.iters if i is None else i
            return n * (4 * x.groups) + (BANKS + 4 * x.g0)

        block = ctx.enter_context(nc.Block())

        @block.sync
        def _(sp):
            def slot_wait(s, i, x):
                if s < SLOTS:
                    return
                def need(s):
                    old = s - SLOTS
                    return {"M": (w_used, nm), "A": (ada_used, na), "W": (w1_used, nw)}[kinds[old]][0], \
                        {"M": nm, "A": na, "W": nw}[kinds[old]][old + 1]
                if isinstance(i, int):
                    who, count = need(s)
                    sp.wait_ge(who, count)
                else:
                    n = len(x.items)
                    (who, c1), (_, c2) = need(s), need(s + n) if x.iters > 2 else need(s)
                    sp.wait_ge(who, (i - 1) * (c2 - c1) + c1)

            def source(x, i, item):
                kind, g, q = item
                l = x.layer
                if kind == "A":
                    c = x.first_chunk + g
                    lc = c // CHUNKS
                    if x.iters > 1:
                        assert (c + (x.iters - 1) * x.chunks) // CHUNKS == lc
                    return rows(w_ada[lc], 4 * q, 4)[:, :, bass.ds(i * (512 * x.chunks) + (c % CHUNKS) * 512, 512)]
                if kind == "W":
                    w = (w_cmp1_k, w_cmp1_v)[q // 2][l]
                    return w[(q % 2) * 16 * P:(q % 2 + 1) * 16 * P, :].rearrange("(j p) n -> p j n", p=P)
                k0, kn = sum(x.ktiles[:q]), x.ktiles[q]
                if x.name == "fox":
                    return rows(w_in[l], k0, kn)[:, :, bass.ds(i * 512, 512)]
                if x.name == "nsa":
                    return rows(w_in[l], k0, kn)[:, :, bass.ds(i * 512 + (FF0 + FOX), 512)]
                if x.name == "out":
                    return rows(w_out[l], k0, kn)[:, :, bass.ds(i * 512, 512)]
                if x.name == "down":
                    return rows(w_down[l], k0, kn)[:, :, bass.ds(i * 512, 512)]
                return [rows(w_up[l], k0, kn)[:, :, bass.ds(i * 512 + (g * 256 + v * FF), 256)] for v in range(2)]

            def stream(x, i):
                n = len(x.items)
                for posn, item in enumerate(x.items):
                    s = x.s0 + (i if isinstance(i, int) else 1) * n + posn
                    slot_wait(s, i, x)
                    slot = s % SLOTS
                    src = source(x, i, item)
                    if isinstance(src, list):
                        parts = [(raw[:, slot, :, v * 256:(v + 1) * 256], src[v]) for v in range(2)]
                    else:
                        n_rows = src.shape[1]
                        dst = raw[:, slot].rearrange("p k (j n) -> p (k j) n", n=P) if item[0] == "W" else raw[:, slot]
                        cut = (n_rows + 1) // 2
                        parts = [(dst[:, 0:cut], src[:, 0:cut]), (dst[:, cut:n_rows], src[:, cut:n_rows])]
                    for d_, s_ in parts:
                        sp.dma_start(d_, s_).then_inc(full[slot], 16)

            sp.dma_start(par_sb[:], par).then_inc(par_loaded, 16)
            for x in phases:
                stream(x, 0)
                if x.name == "pre":
                    sp.dma_start(x_sb[:], xT).then_inc(x_loaded, 16)
                if x.name == "fox":
                    l = x.layer
                    if l:
                        sp.wait_ge(x_done, 2 * l)
                    sp.dma_start(c_sb[:], consts).then_inc(ext_loaded, 16)
                    sp.dma_start(w2[:, 0, :], w_cmp2_k[l]).then_inc(ext_loaded, 16)
                    sp.dma_start(w2[:, 1, :], w_cmp2_v[l]).then_inc(ext_loaded, 16)
                    sp.dma_start(pos_sb[:], pos[l]).then_inc(ext_loaded, 16)
                    sp.dma_start(wx[:, :, 0:FOX], rows(w_in[l], 0, KT)[:, :, FF0:FF0 + FOX]).then_inc(ext_loaded, 16)
                    sp.dma_start(wx[:, :, FOX:32], rows(w_in[l], 0, KT)[:, :, NG0:D_IN]).then_inc(ext_loaded, 16)
                repeat(sp, 1, x.iters, lambda i, x=x: stream(x, i))
            for q in range(4):
                sp.wait_ge(hh_ready, 4 * (2 * DEPTH) + q + 1)
                sp.dma_start(out[:, 4 * q:4 * q + 4, :], nrm[:, 4 * q:4 * q + 4, :]).then_inc(stored, 16)
            sp.wait_ge(stored, 64)

        EXT = 6 * 16

        def arrived(eng, x, i, posn):
            per = len(x.items) // SLOTS
            eng.wait_ge(full[posn % SLOTS], i * (32 * per) + 32 * (x.s0 // SLOTS + posn // SLOTS + 1))

        def m_index(x, i, posn):
            return i * x.m_per + (x.m0 + sum(y[0] == "M" for y in x.items[:posn]))

        def a_index(x, i, posn):
            return i * x.a_per + (x.a0 + sum(y[0] == "A" for y in x.items[:posn]))

        @block.tensor
        def _(pe):
            pe.wait_ge(ones_ready, 1)

            def main_step(x, i, posn):
                _, g, q = x.items[posn]
                m = m_index(x, i, posn)
                mi = sum(y[0] == "M" for y in x.items[:posn])
                pe.wait_ge(lo_ready, m + 1)
                first, last = q == 0, q == len(x.ktiles) - 1
                k0, kn = sum(x.ktiles[:q]), x.ktiles[q]
                rhs = actb if x.name == "down" else hb
                for b in range(BANKS):
                    if first:
                        pe.wait_ge(bank_free, i * (4 * x.groups) + (4 * (x.g0 + g) + b + 1))
                    for k in range(kn):
                        w = slice(b * P, (b + 1) * P)
                        pe.matmul(ps[:, b, :], whi[:, mi % HSLOTS, k, w], rhs[:, k0 + k, :],
                                  start=first and k == 0, stop=False)
                        mm = pe.matmul(ps[:, b, T:2 * T], wlo[:, posn % SLOTS, k, w], rhs[:, k0 + k, 0:T],
                                       start=False, stop=last and k == kn - 1)
                    if last and b < BANKS - 1:
                        mm.then_inc(bank_full, 1)
                mm.then_inc(w_used, 1)

            def ada_total(x, i, posn):
                pe.wait_ge(ada_used, a_index(x, i, posn) + 1)
                for b in range(4):
                    mm = pe.matmul(ps[:, 4, b:b + 1], acc[:, b * P:(b + 1) * P], ones[:, 0:1], start=True, stop=True)
                mm.then_inc(ada_sum, 1)

            def run(x):
                def body(i):
                    for posn, item in enumerate(x.items):
                        if item[0] == "M":
                            main_step(x, i, posn)
                        elif item[0] == "A" and item[2] == 3:
                            ada_total(x, i, posn)
                repeat(pe, 0, x.iters, body)

            def norm(n):
                pe.wait_ge(ss_ready, n + 1)
                pe.matmul(ps[:, 5, 0:T], ones[:], ssum[:], start=True, stop=True).then_inc(ssb_ready, 1)

            ident = c_sb[:, C_ID:C_ID + P]
            neg = c_sb[:, C_NEG:C_NEG + P]

            def attention(l):
                pe.wait_ge(xlo_ready, l + 1)
                for tb in range(TB):
                    for k in range(KT):
                        hi = hb[:, k, tb * P:(tb + 1) * P]
                        lo = hb[:, k, T + tb * P:T + (tb + 1) * P]
                        dst = ps[:, 5, tb * 32:tb * 32 + 32]
                        pe.matmul(dst, hi, wxhi[:, k, :], start=k == 0, stop=False)
                        pe.matmul(dst, hi, wxlo[:, k, :], start=False, stop=False)
                        mm = pe.matmul(dst, lo, wxhi[:, k, :], start=False, stop=k == KT - 1)
                mm.then_inc(ext_sum, 1)
                pe.wait_ge(bank_free, tiles_out(phase("nsa", l)))
                for n, tile in enumerate((ZVS, ZVW)):
                    for g in range(KV):
                        for tb in range(TB):
                            dst = ps[:, 6 + n, (g * TB + tb) * P:(g * TB + tb + 1) * P]
                            mm = pe.transpose(dst, z[:, tile + g, tb * P:(tb + 1) * P], ident)
                mm.then_inc(vsw_t, 1)
                pe.wait_ge(lf_ready, l + 1)
                for tb in range(TB):
                    mm = pe.matmul(ps[0:FOX, 5, P:P + T], lf[:, tb, :], c_sb[:, C_TRI + tb * T:C_TRI + (tb + 1) * T],
                                   start=tb == 0, stop=tb == TB - 1)
                mm.then_inc(cum_ready, 1)
                x = phase("cmp", l)
                for kind in range(2):
                    pe.wait_ge(xb_ready, 2 * l + kind + 1)
                    for half in range(2):
                        arrived(pe, x, 0, 2 * kind + half)
                        for j in range(16):
                            w = raw[:, 2 * kind + half].rearrange("p k (j n) -> p (k j) n", n=P)[:, j, :]
                            mm = pe.matmul(ps[:, kind, 0:KV * NC], w, xb[:, kind, half * 16 + j, :],
                                           start=half == 0 and j == 0, stop=half == 1 and j == 15)
                        mm.then_inc(w1_used, 1)
                    pe.wait_ge(gel_ready, 2 * l + kind + 1)
                    if kind == 0:
                        mm = pe.matmul(ps[:, 2, 0:KV * NC], w2[:, 0, :], gel[:], start=True, stop=True)
                    else:
                        for g in range(KV):
                            mm = pe.matmul(ps[0:NC, 3, g * P:(g + 1) * P], gel[:, g * NC:(g + 1) * NC], w2[:, 1, :],
                                           start=True, stop=True)
                    mm.then_inc(cmp_ready, 1)
                pe.wait_ge(cmpc_ready, 2 * l + 2)
                pe.wait_ge(vsw_ready, l + 1)
                pe.wait_ge(zero_ready, l + 1)
                pe.wait_ge(bias_ready, l + 1)

                def head(h, kv):
                    pe.wait_ge(stage_ready, h + (l * FOX + 1))
                    pe.wait_ge(r_ready, h + (l * FOX + 1))

                    def scores(bank, q, keys, bias):
                        for n, (tb, kb) in enumerate(((0, 0), (1, 0), (1, 1))):
                            dst = ps[:, bank, n * P:(n + 1) * P]
                            diag = tb == kb
                            mm = pe.matmul(dst, q[:, tb * P:(tb + 1) * P], keys[:, kb * P:(kb + 1) * P],
                                           start=True, stop=not (bias or diag))
                            if bias:
                                mm = pe.matmul(dst, Lb[0:40, tb * P:(tb + 1) * P], Rb[0:40, kb * P:(kb + 1) * P],
                                               start=False, stop=not diag)
                            if diag:
                                mm = pe.matmul(dst, ident, neg, start=False, stop=True)
                        mm.then_inc(s_ready, 1)

                    scores(0, qf, flat(z[:, bass.ds(h + ZK, 1), :]), True)
                    for tb in range(TB):
                        mm = pe.matmul(ps[:, 3, tb * 16:tb * 16 + NC], qn[:, tb * P:(tb + 1) * P],
                                       kcT[:, kv * NC:(kv + 1) * NC], start=True, stop=True)
                    mm.then_inc(s_ready, 1)
                    scores(1, qn, z[:, ZKS + kv, :], False)
                    scores(2, qn, z[:, ZKW + kv, :], False)
                    for tb in range(TB):
                        mm = pe.transpose(ps[:, 6, T + tb * P:T + (tb + 1) * P], vfT[:, tb * P:(tb + 1) * P], ident)
                    mm.then_inc(vt_ready, 1)

                    def turn(u):
                        pe.wait_ge(pn_ready, h * 4 + (l * 4 * FOX + u + 1))
                        if u == 1:
                            src = [prc[:, 0, :], prc[:, 1, :]]
                        else:
                            src = [pr[:, u - (u > 0), n * P:(n + 1) * P] for n in range(3)]
                        for n, s in enumerate(src):
                            mm = pe.transpose(ps[:, 4 + u % 2, n * P:(n + 1) * P], s, ident)
                        mm.then_inc(pt_ready, 1)

                    def values(u):
                        pe.wait_ge(ptc_ready, h * 4 + (l * 4 * FOX + u + 1))
                        if u == 0:
                            pe.wait_ge(vf_ready, h + (l * FOX + 1))
                        if u <= 1:
                            pe.wait_ge(o_done, h * 2 + (l * 2 * FOX + u + 1))
                        if u == 1:
                            mm = pe.matmul(ps[:, 7, 0:T], vc[0:NC, kv, :], ptc[0:NC, :], start=True, stop=False)
                        else:
                            v = vf if u == 0 else vsw[:, u - 2, kv]
                            t = pt[:, u - (u > 0)]
                            if u == 0:
                                pe.matmul(ps[:, 6, 0:P], v[:, 0, :], t[:, 0:P], start=True, stop=True)
                                pe.matmul(ps[:, 6, P:T], v[:, 0, :], t[:, P:T], start=True, stop=False)
                                mm = pe.matmul(ps[:, 6, P:T], v[:, 1, :], t[:, T:3 * P], start=False, stop=True)
                            else:
                                pe.matmul(ps[:, 7, P:T], v[:, 1, :], t[:, T:3 * P], start=False, stop=False)
                                mm = pe.matmul(ps[:, 7, 0:T], v[:, 0, :], t[:, 0:T], start=False, stop=u == 3)
                        mm.then_inc(pv_ready, 1)

                    turn(0)
                    turn(1)
                    values(0)
                    turn(2)
                    values(1)
                    turn(3)
                    values(2)
                    values(3)

                for kv in range(KV):
                    repeat(pe, kv * GROUP, (kv + 1) * GROUP, lambda h, kv=kv: head(h, kv))

            run(phase("pre", 0))
            for l in range(DEPTH):
                norm(2 * l)
                pe.wait_ge(h_ready, 4 * (2 * l + 1))
                run(phase("fox", l))
                run(phase("nsa", l))
                run(phase("ext", l))
                attention(l)
                pe.wait_ge(o_done, 2 + 2 * FOX * (l + 1))
                run(phase("out", l))
                norm(2 * l + 1)
                pe.wait_ge(h_ready, 4 * (2 * l + 2))
                run(phase("up", l))
                pe.wait_ge(act_ready, FT // 2 * (l + 1))
                run(phase("down", l))
            norm(2 * DEPTH)

        @block.scalar
        def _(act):
            own = Chain(act, act_own)
            act.wait_ge(par_loaded, 16)
            act.activation(cact[:], par_sb[:, V_C:V_C + KT], ACT.Silu).then_inc(cact_ready, 1)

            def split_hi(x, i, posn):
                mi = sum(y[0] == "M" for y in x.items[:posn])
                kn = x.ktiles[x.items[posn][2]]
                arrived(act, x, i, posn)
                if not (isinstance(i, int) and i == 0 and x.m0 + mi < HSLOTS):
                    act.wait_ge(w_used, i * x.m_per + (x.m0 + mi - HSLOTS + 1))
                act.activation(whi[:, mi % HSLOTS, 0:kn, :], raw[:, posn % SLOTS, 0:kn, :], ACT.Copy)\
                   .then_inc(hi_ready, 1)

            def full_bank(x, i, g, b):
                if b < BANKS - 1:
                    act.wait_ge(bank_full, i * (3 * x.groups) + (3 * (x.g0 + g) + b + 1))
                else:
                    act.wait_ge(w_used, i * x.m_per + (x.m0 + (g + 1) * (x.m_per // x.groups)))

            def out_plain(x, i, g, stage):
                if stage:
                    return
                for b in range(BANKS):
                    full_bank(x, i, g, b)
                    act.wait_ge(bank_free, i * (4 * x.groups) + (4 * (x.g0 + g) + b + 1))
                    act.activation(evb[:, b, :], ps[:, b, T:2 * T], ACT.Copy).then_inc(half_out, 1)

            def conv_col(l, tile, n):
                return par_sb[:, bass.ds(tile * 3 + (l * V_L + V_CW + n), 1)]

            def out_conv(x, i, g, stage):
                l = x.layer
                G = i * x.groups + g
                n0 = (x.layer) * (FT // 2)
                if stage == 0:
                    for b in range(BANKS):
                        full_bank(x, i, g, b)
                        act.wait_ge(conv_done, G * 1 + (n0 + 1))
                        act.activation(ub[:, b, 2:T + 2], ps[:, b, T:2 * T], ACT.Copy).then_inc(half_out, 1)
                elif stage == 1:
                    for b in range(BANKS):
                        tile = G * 2 + (b % 2 + (b // 2) * FT)
                        act.wait_ge(bank_free, i * (4 * x.groups) + (BANKS + 4 * (x.g0 + g) + b + 1))
                        act.activation(yb[:, b, :], ub[:, b, 2:T + 2], ACT.Identity,
                                       bias=par_sb[:, bass.ds(tile + (l * V_L + V_CB), 1)],
                                       scale=conv_col(l, tile, 2)).then_inc(conv_y, 1)
                elif stage == 2:
                    act.wait_ge(conv_done, G * 1 + (n0 + 2))
                    act.activation(yb[:, 0:2, :], yb[:, 0:2, :], ACT.Silu).then_inc(silu_done, 1)
                else:
                    act.wait_ge(prod_done, G * 1 + (n0 + 1))
                    act.activation(actb[:, bass.ds(G * 2, 2), 0:T], sb_[:], ACT.Copy).then_inc(acthi, 1)

            def run(x):
                evac = out_conv if x.name == "up" else out_plain

                def body(i, first):
                    for posn, item in enumerate(x.items):
                        if item[0] == "M":
                            split_hi(x, i, posn)
                            _, g, q = item
                            if q < 4 and not (first and g == 0):
                                if g == 0:
                                    evac(x, i - 1, x.groups - 1, q)
                                else:
                                    evac(x, i, g - 1, q)
                if x.m_per:
                    body(0, True)
                    repeat(act, 1, x.iters, lambda i: body(i, False))
                    for stage in range(4):
                        evac(x, x.iters - 1, x.groups - 1, stage)

            def norm(n):
                final = n == 2 * DEPTH
                l = n // 2
                if n:
                    act.wait_ge(x_done, n)
                else:
                    act.wait_ge(x_loaded, 16)
                for q in range(4):
                    act.activation(nrm[:, 4 * q:4 * q + 4, :], x_sb[:, 4 * q:4 * q + 4, :], ACT.Square).then_inc(sq_ready, 1)
                act.wait_ge(var_ready, n + 1)
                act.activation(rstd[:], ssum[:], ACT.Sqrt).then_inc(root_ready, 1)
                shift = M_SHF if n % 2 else M_SHA
                for q in range(4):
                    act.wait_ge(t_ready, 4 * n + q + 1)
                    for k in range(4 * q, 4 * q + 4):
                        if final:
                            a = act.activation(nrm[:, k, :], nrm[:, k, :], ACT.Copy, scale=par_sb[:, V_FIN + k:V_FIN + k + 1])
                        else:
                            a = act.activation(nrm[:, k, :], nrm[:, k, :], ACT.Identity, bias=modc(l, shift + k),
                                               scale=acol[:, k:k + 1])
                    a.then_inc(hh_ready, 1)
                    if not final:
                        act.wait_ge(hh_ready, 4 * n + q + 1)
                        act.activation(hb[:, 4 * q:4 * q + 4, 0:T], nrm[:, 4 * q:4 * q + 4, :], ACT.Copy)\
                           .then_inc(hhi_ready, 1)

            def attention(l):
                act.wait_ge(ext_loaded, EXT * (l + 1))
                act.activation(wxhi[:], wx[:], ACT.Copy).then_inc(xhi_ready, 1)
                act.wait_ge(vsw_t, l + 1)
                for n in range(2):
                    a = act.activation(vsw[:, n].rearrange("p g t d -> p (g t d)"), ps[:, 6 + n, :], ACT.Copy)
                a.then_inc(vsw_ready, 1)
                act.wait_ge(lg_ready, l + 1)
                own(act.activation(ln1[:], lg[:, :, 0:FOX], ACT.Abs))
                own(act.activation(ln1[:], ln1[:], ACT.Exp, scale=-1.0))
                act.activation(eg[:, :, FOX:32], lg[:, :, FOX:32], ACT.Exp, scale=-1.0)
                act.activation(ln1[:], ln1[:], ACT.Ln, bias=1.0).then_inc(eg_ready, 1)
                for kind in range(2):
                    act.wait_ge(w1_used, 4 * l + 2 * kind + 2)
                    act.activation(gel[:], ps[:, kind, 0:KV * NC], ACT.Gelu_apprx_tanh).then_inc(gel_ready, 1)

                def head(h):
                    def expo(u):
                        act.wait_ge(nb_ready, h * 4 + (l * 4 * FOX + u + 1))
                        if u == 1:
                            a = act.activation(sc[:, :, 0:NC], sc[:, :, 0:NC], ACT.Exp, scale=SCALE)
                        else:
                            n = u - (u > 0)
                            bank = (0, 3, 1, 2)[u]
                            act.activation(pr[:, n, 0:P], ps[:, bank, 0:P], ACT.Exp, bias=nb[:, u, 0:1],
                                           scale=SCALE, accum_out=rs[:, u, 0:1])
                            a = act.activation(pr[:, n, P:3 * P], ps[:, bank, P:3 * P], ACT.Exp, bias=nb[:, u, 1:2],
                                               scale=SCALE, accum_out=rs[:, u, 1:2])
                        a.then_inc(p_ready, 1)

                    def copy(u):
                        act.wait_ge(pt_ready, h * 4 + (l * 4 * FOX + u + 1))
                        if u == 1:
                            a = act.activation(ptc[:], ps[:, 5, 0:TB * P], ACT.Copy)
                        else:
                            a = act.activation(pt[:, u - (u > 0), :], ps[:, 4 + u % 2, 0:3 * P], ACT.Copy)
                        a.then_inc(ptc_ready, 1)

                    def high(n):
                        act.wait_ge(pv_ready, h * 4 + (l * 4 * FOX + (1 if n == 0 else 4)))
                        act.activation(flat(hb[:, bass.ds(h + n * FOX, 1), 0:T]), ps[:, 6 + n, 0:T], ACT.Copy)\
                           .then_inc(ohi_ready, 1)

                    act.wait_ge(vt_ready, h + (l * FOX + 1))
                    act.activation(vf[:].rearrange("p t d -> p (t d)"), ps[:, 6, T:2 * T], ACT.Copy).then_inc(vf_ready, 1)
                    expo(0)
                    expo(1)
                    copy(0)
                    expo(2)
                    copy(1)
                    expo(3)
                    copy(2)
                    high(0)
                    copy(3)
                    high(1)

                repeat(act, 0, FOX, head)

            for l in range(DEPTH):
                norm(2 * l)
                run(phase("fox", l))
                run(phase("nsa", l))
                attention(l)
                run(phase("out", l))
                norm(2 * l + 1)
                run(phase("up", l))
                run(phase("down", l))
            norm(2 * DEPTH)

        @block.vector
        def _(dve):
            own = Chain(dve, dve_own)
            dve.sem_inc(bank_free, BANKS)
            dve.sem_inc(conv_done, 1)
            dve.sem_inc(o_done, 2)
            dve.memset(ones[:], 1.0).then_inc(ones_ready, 1)
            dve.wait_ge(cact_ready, 1)

            def split_lo(x, i, posn):
                kn = x.ktiles[x.items[posn][2]]
                mi = sum(y[0] == "M" for y in x.items[:posn])
                slot = posn % SLOTS
                dve.wait_ge(hi_ready, m_index(x, i, posn) + 1)
                dve.tensor_tensor(wlo[:, slot, 0:kn, :], raw[:, slot, 0:kn, :],
                                  whi[:, mi % HSLOTS, 0:kn, :].bitcast(F32), ALU.subtract).then_inc(lo_ready, 1)

            def ada_step(x, i, posn):
                r = x.items[posn][2]
                slot = posn % SLOTS
                arrived(dve, x, i, posn)
                for k in range(4):
                    kt = 4 * r + k
                    c = cact[:, kt:kt + 1]
                    if kt == 0:
                        a = dve.tensor_scalar(acc[:], raw[:, slot, k, :], c, None, ALU.mult)
                    else:
                        a = dve.scalar_tensor_tensor(out=acc[:], in0=raw[:, slot, k, :], scalar=c, in1=acc[:],
                                                     op0=ALU.mult, op1=ALU.add)
                    if k < 3:
                        own(a)
                a.then_inc(ada_used, 1)
                dve.wait_ge(ada_used, a_index(x, i, posn) + 1)

            def ada_out(x, i, c):
                first = x.first_chunk + c
                l = first // CHUNKS
                dve.wait_ge(ada_sum, i * x.chunks + (first + 1))
                col = i * (4 * x.chunks) + (first % CHUNKS) * 4
                own(dve.tensor_tensor(mod[:, l, bass.ds(col, 4)], ps[:, 4, 0:4],
                                      par_sb[:, bass.ds(col + (l * V_L + V_BA), 4)], ALU.add))

            def out_plain(x, i, g, stage):
                if stage:
                    return
                l = x.layer
                for b in range(BANKS):
                    n = i * (4 * x.groups) + (4 * (x.g0 + g) + b + 1)
                    dve.wait_ge(half_out, n)
                    tile = i * 4 + b
                    if x.name in ("fox", "nsa"):
                        at_ = tile + (ZNQ if x.name == "nsa" else 0)
                        dve.tensor_tensor(flat(z[:, bass.ds(at_, 1), :]), ps[:, b, 0:T], evb[:, b, :], ALU.add)\
                           .then_inc(bank_free, 1)
                    else:
                        own(dve.tensor_tensor(evb[:, b, :], ps[:, b, 0:T], evb[:, b, :], ALU.add))
                        gate_ = mod[:, l, bass.ds(tile + (M_GA if x.name == "out" else M_GF), 1)]
                        xt = flat(x_sb[:, bass.ds(tile, 1), :])
                        dve.scalar_tensor_tensor(out=xt, in0=evb[:, b, :], scalar=gate_, in1=xt,
                                                 op0=ALU.mult, op1=ALU.add).then_inc(bank_free, 1)

            def conv_col(l, tile, n):
                return par_sb[:, bass.ds(tile * 3 + (l * V_L + V_CW + n), 1)]

            def out_conv(x, i, g, stage):
                l = x.layer
                G = i * x.groups + g
                n0 = l * (FT // 2)
                if stage == 0:
                    for b in range(BANKS):
                        n = i * (4 * x.groups) + (4 * (x.g0 + g) + b + 1)
                        dve.wait_ge(half_out, n)
                        u = ub[:, b, 2:T + 2]
                        dve.tensor_tensor(u, ps[:, b, 0:T], u, ALU.add).then_inc(bank_free, 1)
                elif stage == 1:
                    for tap in (1, 0):
                        for b in range(BANKS):
                            tile = G * 2 + (b % 2 + (b // 2) * FT)
                            if tap == 1:
                                dve.wait_ge(conv_y, G * 4 + (4 * n0 + b + 1))
                            a = dve.scalar_tensor_tensor(out=yb[:, b, :], in0=ub[:, b, tap:T + tap],
                                                         scalar=conv_col(l, tile, tap), in1=yb[:, b, :],
                                                         op0=ALU.mult, op1=ALU.add)
                            if tap == 1:
                                if b == BANKS - 1:
                                    own(a)
                            elif b == BANKS - 1:
                                a.then_inc(conv_done, 1)
                elif stage == 2:
                    dve.wait_ge(silu_done, G * 1 + (n0 + 1))
                    dve.tensor_tensor(sb_[:], yb[:, 0:2, :], yb[:, 2:4, :], ALU.mult).then_inc(prod_done, 1)
                else:
                    dve.wait_ge(acthi, G * 1 + (n0 + 1))
                    hi = actb[:, bass.ds(G * 2, 2), 0:T]
                    dve.tensor_tensor(actb[:, bass.ds(G * 2, 2), T:2 * T], sb_[:], hi.bitcast(F32), ALU.subtract)\
                       .then_inc(act_ready, 1)
                    dve.wait_ge(act_ready, G * 1 + (n0 + 1))

            def run(x):
                evac = out_conv if x.name == "up" else out_plain
                if not x.m_per:
                    def only(i):
                        for posn, item in enumerate(x.items):
                            if item[0] == "A":
                                ada_step(x, i, posn)
                                if item[2] == 3:
                                    ada_out(x, i, item[1])
                    if x.a_per:
                        own.loop(0, x.iters, 13 * x.chunks, only)
                    return
                per = 13 * x.chunks
                if x.name in ("out", "down"):
                    per += 4
                if x.name == "up":
                    per += x.groups

                def body(i, first):
                    pending = None if first or not x.chunks else (i - 1, x.chunks - 1)
                    for posn, item in enumerate(x.items):
                        if item[0] == "M":
                            split_lo(x, i, posn)
                            _, g, q = item
                            if q < 4 and not (first and g == 0):
                                if g == 0:
                                    evac(x, i - 1, x.groups - 1, q)
                                else:
                                    evac(x, i, g - 1, q)
                            if pending:
                                ada_out(x, *pending)
                                pending = None
                        else:
                            ada_step(x, i, posn)
                            if item[2] == 3:
                                pending = (i, item[1])
                    assert pending is None or pending[1] == x.chunks - 1

                body(0, True)
                own.loop(1, x.iters, per, lambda i: body(i, False))
                for stage in range(4):
                    evac(x, x.iters - 1, x.groups - 1, stage)
                if x.chunks:
                    ada_out(x, x.iters - 1, x.chunks - 1)

            def norm(n):
                final = n == 2 * DEPTH
                l = n // 2
                dve.wait_ge(sq_ready, 4 * n + 4)
                dve.tensor_reduce(ssum[:], nrm[:].rearrange("p k t -> p t k"), AX.X, ALU.add).then_inc(ss_ready, 1)
                if not final:
                    gain = V_GF if n % 2 else V_GA
                    scl = M_SCF if n % 2 else M_SCA
                    own(dve.scalar_tensor_tensor(out=acol[:], in0=mod[:, l, scl:scl + KT], scalar=1.0,
                                                 in1=par_sb[:, l * V_L + gain:l * V_L + gain + KT],
                                                 op0=ALU.add, op1=ALU.mult))
                dve.wait_ge(ssb_ready, n + 1)
                dve.tensor_scalar(ssum[:], ps[:, 5, 0:T], 1.0 / D, EPS, ALU.mult, ALU.add).then_inc(var_ready, 1)
                dve.wait_ge(root_ready, n + 1)
                own(dve.reciprocal(rstd[:], rstd[:]))
                for q in range(4):
                    dve.tensor_tensor(nrm[:, 4 * q:4 * q + 4, :], x_sb[:, 4 * q:4 * q + 4, :],
                                      rstd[:].unsqueeze(1).broadcast_to([P, 4, T]), ALU.mult).then_inc(t_ready, 1)
                    if not final and q:
                        low(n, q - 1)
                if not final:
                    low(n, 3)

            def low(n, q):
                dve.wait_ge(hhi_ready, 4 * n + q + 1)
                hi = hb[:, 4 * q:4 * q + 4, 0:T].bitcast(F32)
                dve.tensor_tensor(hb[:, 4 * q:4 * q + 4, T:2 * T], nrm[:, 4 * q:4 * q + 4, :], hi, ALU.subtract)\
                   .then_inc(h_ready, 1)

            def rope(t0, n):
                zz = z[:, t0:t0 + n, :]
                half = HD // 2
                for a, b in ((0, half), (half, 0)):
                    sin = c_sb[b:b + half, C_SIN:C_SIN + T].unsqueeze(1).broadcast_to([half, n, T])
                    last = dve.tensor_tensor(rtmp[a:a + half, 0:n, :], z[b:b + half, t0:t0 + n, :], sin, ALU.mult)
                    own(last)
                cos = c_sb[:, C_COS:C_COS + T].unsqueeze(1).broadcast_to([P, n, T])
                own(dve.tensor_tensor(zz, zz, cos, ALU.mult))
                own(dve.tensor_tensor(zz, zz, rtmp[:, 0:n, :], ALU.add))

            def blocks(kind, l):
                for g in range(KV):
                    tile = z[:, (ZVC if kind else ZKC) + g, :]
                    for half in range(2):
                        src = tile[:, half * 16:half * 16 + NC * CS].rearrange("p (n j) -> p j n", j=CS)
                        ps_ = pos_sb[:, kind, half * 16:half * 16 + 16].unsqueeze(2).broadcast_to([P, 16, NC])
                        a = dve.tensor_tensor(xb[:, kind, half * 16:half * 16 + 16, g * NC:(g + 1) * NC], src, ps_, ALU.add)
                a.then_inc(xb_ready, 1)

            def attention(l):
                dve.wait_ge(xhi_ready, l + 1)
                dve.tensor_tensor(wxlo[:], wx[:], wxhi[:].bitcast(F32), ALU.subtract).then_inc(xlo_ready, 1)
                dve.wait_ge(bank_free, tiles_out(phase("nsa", l)))
                blocks(1, l)
                dve.wait_ge(ext_sum, l + 1)
                e = ps[:, 5, 0:64].rearrange("p (t n) -> p t n", t=TB)
                bf = par_sb[:, l * V_L + V_BF:l * V_L + V_BF + FOX].unsqueeze(1).broadcast_to([P, TB, FOX])
                dve.tensor_tensor(lg[:, :, 0:FOX], e[:, :, 0:FOX], bf, ALU.add)
                dve.tensor_scalar(lg[:, :, FOX:32], e[:, :, FOX:32], 1.0, None, ALU.mult).then_inc(lg_ready, 1)
                rope(ZKC, KV)
                blocks(0, l)
                dve.wait_ge(eg_ready, l + 1)
                own(dve.tensor_scalar(gate[:], eg[:, :, FOX:32], 1.0, None, ALU.add))
                own(dve.reciprocal(gate[:], gate[:]))
                own(dve.tensor_scalar(lf[:], lg[:, :, 0:FOX], 0.0, ROOT, ALU.min, ALU.mult))
                dve.scalar_tensor_tensor(out=lf[:], in0=ln1[:], scalar=-ROOT, in1=lf[:], op0=ALU.mult, op1=ALU.add)\
                   .then_inc(lf_ready, 1)
                rope(ZKS, KV)
                rope(ZKW, KV)
                rope(ZNQ, NSA)
                dve.wait_ge(cum_ready, l + 1)
                dve.wait_ge(zero_ready, l + 1)
                cum = ps[0:FOX, 5, P:P + T]
                own(dve.tensor_scalar(Rall[0:FOX, :], cum, -1.0, None, ALU.mult))
                dve.tensor_scalar(Lb[32:32 + FOX, :], cum, 1.0, None, ALU.mult).then_inc(bias_ready, 1)
                dve.wait_ge(cmp_ready, 2 * l + 1)
                dve.tensor_copy(kcT[:], ps[:, 2, 0:KV * NC]).then_inc(cmpc_ready, 1)
                dve.wait_ge(cmp_ready, 2 * l + 2)
                dve.tensor_copy(vc[0:NC].rearrange("p g d -> p (g d)"), ps[0:NC, 3, 0:KV * P]).then_inc(cmpc_ready, 1)

                cneg = c_sb[:, C_CNEG:C_CNEG + 32].rearrange("p (t n) -> p t n", t=TB)[:, :, 0:NC]
                c01 = c_sb[:, C_C01:C_C01 + 32].rearrange("p (t n) -> p t n", t=TB)[:, :, 0:NC]

                def head(h):
                    dve.tensor_scalar(Rb[0:40, :], Rall[0:40, :], c_sb[0:40, bass.ds(h + C_SEL, 1)], None, ALU.mult)\
                       .then_inc(r_ready, 1)

                    def top(u):
                        dve.wait_ge(s_ready, h * 4 + (l * 4 * FOX + u + 1))
                        bank = (0, 3, 1, 2)[u]
                        if u == 1:
                            s = ps[:, bank, 0:32].rearrange("p (t n) -> p t n", t=TB)[:, :, 0:NC]
                            own(dve.tensor_tensor(sc[:, :, 0:NC], s, cneg, ALU.add))
                            own(dve.tensor_reduce(mx[:, u, :], sc[:, :, 0:NC], AX.X, ALU.max))
                            for tb in range(TB):
                                a = dve.tensor_scalar(sc[:, tb, 0:NC], sc[:, tb, 0:NC], mx[:, u, tb:tb + 1], None, ALU.subtract)
                            a.then_inc(nb_ready, 1)
                        else:
                            dve.tensor_reduce(mx[:, u, 0:1], ps[:, bank, 0:P], AX.X, ALU.max)
                            own(dve.tensor_reduce(mx[:, u, 1:2], ps[:, bank, P:3 * P], AX.X, ALU.max))
                            dve.tensor_scalar(nb[:, u, :], mx[:, u, :], -SCALE, None, ALU.mult).then_inc(nb_ready, 1)

                    def scale(u):
                        dve.wait_ge(p_ready, h * 4 + (l * 4 * FOX + u + 1))
                        if u == 1:
                            own(dve.tensor_tensor(sc[:, :, 0:NC], sc[:, :, 0:NC], c01, ALU.mult))
                            own(dve.tensor_reduce(rs[:, u, :], sc[:, :, 0:NC], AX.X, ALU.add))
                        own(dve.tensor_scalar(rr[:, u, :], rs[:, u, :], TINY, None, ALU.max))
                        own(dve.reciprocal(rr[:, u, :], rr[:, u, :]))
                        if u:
                            g = gate[:, :, bass.ds(h * 3 + (u - 1), 1)].rearrange("p t n -> p (t n)")
                            own(dve.tensor_tensor(rr[:, u, :], rr[:, u, :], g, ALU.mult))
                        for tb in range(TB):
                            r = rr[:, u, tb:tb + 1]
                            if u == 1:
                                a = dve.tensor_scalar(prc[:, tb, 0:NC], sc[:, tb, 0:NC], r, None, ALU.mult)
                            else:
                                cols = pr[:, u - (u > 0), 0:P] if tb == 0 else pr[:, u - (u > 0), P:3 * P]
                                a = dve.tensor_scalar(cols, cols, r, None, ALU.mult)
                        a.then_inc(pn_ready, 1)

                    def low_(n):
                        dve.wait_ge(ohi_ready, h * 2 + (l * 2 * FOX + n + 1))
                        tile = bass.ds(h + n * FOX, 1)
                        dve.tensor_tensor(flat(hb[:, tile, T:2 * T]), ps[:, 6 + n, 0:T], flat(hb[:, tile, 0:T]).bitcast(F32),
                                          ALU.subtract).then_inc(o_done, 1)

                    top(0)
                    top(1)
                    scale(0)
                    top(2)
                    scale(1)
                    top(3)
                    scale(2)
                    scale(3)
                    low_(0)
                    low_(1)

                own.loop(0, FOX, 18, head)

            run(phase("pre", 0))
            for l in range(DEPTH):
                norm(2 * l)
                run(phase("fox", l))
                run(phase("nsa", l))
                run(phase("ext", l))
                attention(l)
                run(phase("out", l))
                dve.wait_ge(bank_free, tiles_out(phase("out", l)))
                dve.sem_inc(x_done, 1)
                norm(2 * l + 1)
                own(dve.memset(ub[:, :, 0:2], 0.0))
                run(phase("up", l))
                run(phase("down", l))
                dve.wait_ge(bank_free, tiles_out(phase("down", l)))
                dve.sem_inc(x_done, 1)
            norm(2 * DEPTH)

        @block.gpsimd
        def _(pool):
            own = Chain(pool, pool_own)
            for l in range(DEPTH):
                pool.wait_ge(bank_free, tiles_out(phase("nsa", l)))
                own(pool.memset(Lb[:], 0.0))
                own(pool.memset(Rall[:], 0.0))
                pool.memset(Lb[0:FOX, :], 1.0)
                pool.memset(Rall[32:32 + FOX, :], 1.0).then_inc(zero_ready, 1)

                def stage(h):
                    pool.tensor_copy(qf[:], flat(z[:, bass.ds(h + ZQ, 1), :]))
                    pool.tensor_copy(vfT[:], flat(z[:, bass.ds(h + ZV, 1), :]))
                    pool.tensor_copy(qn[:], flat(z[:, bass.ds(h + ZNQ, 1), :])).then_inc(stage_ready, 1)

                pool.wait_ge(bias_ready, l + 1)
                pool.wait_ge(cmp_ready, 2 * l + 2)
                own(pool.memset(prc[:], 0.0))
                stage(0)

                def following(h):
                    pool.wait_ge(vt_ready, h + (l * FOX + 1))
                    stage(h + 1)

                repeat(pool, 0, FOX - 1, following)


_OUT = (P, KT, T)


def kernel(**inputs):
    import numpy as _np
    import concourse.bacc as _bacc
    from concourse import mybir as _mybir
    from concourse.bass_utils import run_bass_kernel_spmd as _run

    g = {k: _np.asarray(v) for k, v in inputs.items()}

    def cols(a, *tail):
        a = a.reshape((a.shape[0], -1, P) + tail)
        return _np.moveaxis(a, 2, 0)

    def per_layer(a):
        return a.reshape(P, DEPTH, -1)

    par = _np.concatenate([
        per_layer(cols(g["attn_norm_g"])),
        per_layer(cols(g["ffn_norm_g"])),
        per_layer(cols(g["b_ada"])),
        per_layer(cols(_np.ascontiguousarray(_np.moveaxis(g["conv_w"], 1, 2)), 3)),
        per_layer(cols(g["conv_b"])),
        _np.broadcast_to(g["b_fgate"][None], (P, DEPTH, FOX)),
    ], axis=2).reshape(P, -1)
    par = _np.concatenate([par, g["final_norm_g"].reshape(KT, P).T, g["c"].reshape(KT, P).T], axis=1)
    pos = _np.stack([g["cmp_pos_k"], g["cmp_pos_v"]], axis=1).transpose(0, 3, 1, 2)
    arrays = {
        "xT": g["x"][0].T.reshape(KT, P, T).transpose(1, 0, 2),
        "par": par,
        "pos": pos,
        "consts": constants(),
    }
    for name in ("w_ada", "w_in", "w_cmp1_k", "w_cmp1_v", "w_cmp2_k", "w_cmp2_v", "w_out", "w_up", "w_down"):
        arrays[name] = g[name]
    arrays = {f"in_{k}": _np.ascontiguousarray(v) for k, v in arrays.items()}
    nc = _bacc.Bacc("TRN2", target_bir_lowering=False, num_devices=1)
    args = [nc.dram_tensor(k, v.shape, _mybir.dt.from_np(v.dtype), kind="ExternalInput").ap()
            for k, v in arrays.items()]
    args.append(nc.dram_tensor("out_T", _OUT, _mybir.dt.float32, kind="ExternalOutput").ap())
    trunk(nc, *args)
    r = _run(nc, [arrays], core_ids=[0])
    got = r.results[0]["out_T"]
    return _np.ascontiguousarray(got.transpose(2, 1, 0).reshape(1, T, D))
```

```python
from contextlib import ExitStack

import numpy as np
import concourse.bass as bass
from concourse import mybir

ALU = mybir.AluOpType
ACT = mybir.ActivationFunctionType
AX = mybir.AxisListType
F32 = mybir.dt.float32
F32R = mybir.dt.float32r

P = 128
D = 2048
T = 256
TB = T // P
KT = D // P
DEPTH = 2
HD = 128
FOX = 8
NSA = 8
KV = 2
GROUP = NSA // KV
FF = 5632
FT = FF // P
D_IN = 3 * FOX * HD + FOX + NSA * HD + 6 * KV * HD + 3 * NSA
NG0 = D_IN - 3 * NSA
FF0 = 3 * FOX * HD
CB, CS = 32, 16
NC = (T - CB) // CS + 1
SCALE = 1.0 / float(np.sqrt(HD))
ROOT = float(np.sqrt(HD))
EPS = 1e-6
NEG = -1e30
TINY = 1e-30

ZQ, ZK, ZV = 0, FOX, 2 * FOX
ZNQ = 3 * FOX
ZKC, ZVC, ZKS, ZVS, ZKW, ZVW = (ZNQ + NSA + KV * n for n in range(6))
ZT = ZNQ + NSA + 6 * KV

SLOTS = 4
ASLOTS = 4
HSLOTS = 2
BANKS = 4
CHUNKS = 6 * D // 512

V_GA, V_GF, V_BA = 0, KT, 2 * KT
V_CW = V_BA + 6 * KT
V_CB = V_CW + 2 * FT * 3
V_BF = V_CB + 2 * FT
V_L = V_BF + FOX
V_FIN = DEPTH * V_L
V_C = V_FIN + KT
V_N = V_C + KT
M_SHA, M_SCA, M_GA, M_SHF, M_SCF, M_GF = (KT * n for n in range(6))

C_ID = 0
C_NEG = C_ID + P
C_TRI = C_NEG + P
C_COS = C_TRI + TB * T
C_SIN = C_COS + T
C_CNEG = C_SIN + T
C_C01 = C_CNEG + TB * 16
C_SEL = C_C01 + TB * 16
C_N = C_SEL + FOX


def constants():
    c = np.zeros((P, C_N), np.float32)
    p = np.arange(P)
    t = np.arange(T)
    c[:, C_ID:C_ID + P] = np.eye(P)
    c[:, C_NEG:C_NEG + P] = np.where(p[None, :] <= p[:, None], 0.0, NEG)
    for b in range(TB):
        c[:, C_TRI + b * T:C_TRI + (b + 1) * T] = t[None, :] >= b * P + p[:, None]
        seen = np.arange(NC)[None, :] * CS + CB - 1 <= (b * P + p)[:, None]
        c[:, C_CNEG + b * 16:C_CNEG + b * 16 + NC] = np.where(seen, 0.0, NEG)
        c[:, C_C01 + b * 16:C_C01 + b * 16 + NC] = seen
    half = HD // 2
    inv = np.float32(10000.0) ** (-np.arange(0, HD, 2, dtype=np.float32) / np.float32(HD))
    ang = (t.astype(np.float32)[:, None] * inv[None, :]).astype(np.float32).T
    c[:, C_COS:C_COS + T] = np.concatenate([np.cos(ang), np.cos(ang)])
    c[:half, C_SIN:C_SIN + T] = np.sin(ang)
    c[half:, C_SIN:C_SIN + T] = -np.sin(ang)
    for h in range(FOX):
        c[h, C_SEL + h] = 1.0
        c[32 + h, C_SEL + h] = 1.0
    return c


class Phase:

    def __init__(self, name, layer, iters, items, groups=0, ktiles=(), src=None, first_chunk=0):
        self.name, self.layer, self.iters, self.items = name, layer, iters, items
        self.groups, self.ktiles, self.src, self.first_chunk = groups, ktiles, src, first_chunk
        self.m_per = sum(x[0] == "M" for x in items)
        self.a_per = sum(x[0] == "A" for x in items)
        self.r_per = len(items) - self.a_per
        self.chunks = self.a_per // KT


def weave(groups, steps, adas):
    out, a = [], 0
    for g in range(groups):
        for q in range(steps):
            out.append(("M", g, q))
            for _ in range(adas):
                out.append(("A", a // KT, a % KT))
                a += 1
    return out


def plan():
    four = (4, 4, 4, 4)
    down = (4,) * 8 + (3,) * 4
    only = [("A", 0, r) for r in range(KT)]
    w1 = [("W", 0, r) for r in range(4)]
    ph, chunk = [], 0

    def add(name, layer, iters, items, **k):
        nonlocal chunk
        x = Phase(name, layer, iters, items, first_chunk=chunk, **k)
        chunk += x.chunks * iters
        ph.append(x)

    for l in range(DEPTH):
        a = 4 if l == 0 else 0
        if l == 0:
            add("pre", l, 8, only)
        add("fox", l, 6, weave(1, 4, a), groups=1, ktiles=four)
        add("nsa", l, 5, weave(1, 4, a), groups=1, ktiles=four)
        add("ext", l, 1, only)
        add("cmp", l, 1, w1)
        add("out", l, 4, weave(1, 4, a), groups=1, ktiles=four)
        add("up", l, 11, weave(2, 4, a // 2), groups=2, ktiles=four)
        add("down", l, 4, weave(1, 12, a), groups=1, ktiles=down)
    assert chunk == DEPTH * CHUNKS
    s = m = a = g = w = r = 0
    kinds = []
    for x in ph:
        x.s0, x.m0, x.a0, x.g0, x.r0 = s, m, a, g, r
        assert s % SLOTS == 0 and x.r_per % SLOTS == 0 and x.a_per % ASLOTS == 0
        kinds += [y[0] for y in x.items if y[0] != "A"] * x.iters
        s += x.r_per * x.iters
        r += BANKS * x.iters * (x.name in ("out", "down"))
        m += x.m_per * x.iters
        a += x.a_per * x.iters
        g += x.groups * x.iters
    return ph, kinds


def repeat(eng, start, end, body):
    if end - start == 1:
        body(start)
    elif end > start:
        with eng.Fori(start, end) as i:
            body(i)


class Chain:

    def __init__(self, eng, sem):
        self.eng, self.sem, self.base, self.k, self.i, self.per = eng, sem, 0, 0, None, 0

    def __call__(self, ins):
        ins.then_inc(self.sem, 1)
        self.k += 1
        at = self.base + self.k if self.i is None else self.i * self.per + (self.base + self.k)
        self.eng.wait_ge(self.sem, at)

    def loop(self, start, end, per, body):
        self.base, self.k = self.base + self.k, 0

        def one(i):
            self.i, self.per, self.k = i, per, 0
            self.base -= start * per
            body(i)
            self.base += start * per
            assert self.k == per, (self.k, per)

        repeat(self.eng, start, end, one)
        self.i, self.k = None, 0
        self.base += per * (end - start)


def trunk(nc, xT, par, pos, consts, w_ada, w_in, w_cmp1_k, w_cmp1_v, w_cmp2_k, w_cmp2_v,
          w_out, w_up, w_down, out):
    phases, kinds = plan()
    nm = [0]
    nw = [0]
    for k in kinds:
        nm.append(nm[-1] + (k == "M"))
        nw.append(nw[-1] + (k == "W"))

    def phase(name, l):
        return next(x for x in phases if x.name == name and x.layer == l)

    with ExitStack() as ctx:
        at = [(nc.sbuf_base + 31) // 32 * 32]

        def place(name, shape, dt=F32, offset=None):
            size = int(np.prod(shape[1:])) * 4
            if offset is None:
                offset = at[0]
                at[0] += (size + 31) // 32 * 32
            return nc.alloc_sbuf_tensor_at(name, shape, dt, offset=offset)

        def end_of(offset, shape):
            return offset + (int(np.prod(shape[1:])) * 4 + 31) // 32 * 32

        x_sb = place("x_sb", [P, KT, T])
        hb = place("hb", [P, KT, 2 * T], F32R)
        whi = place("whi", [P, HSLOTS, 4, 512], F32R)
        ring = at[0]
        raw = place("raw", [P, SLOTS, 4, 512])
        wlo = place("wlo", [P, SLOTS, 4, 512], F32R, offset=ring)
        par_sb = place("par_sb", [P, V_N])
        mod = place("mod", [P, DEPTH, 6 * KT])
        ones = place("ones", [P, P])
        acc = place("acc", [P, 512])
        cact = place("cact", [P, KT])
        acol = place("acol", [P, KT])
        ada_raw = place("ada_raw", [P, ASLOTS, 512])
        scratch = at[0]
        ub = place("ub", [P, 4, T + 2])
        ssum = place("ssum", [P, T], offset=scratch)
        scratch = at[0]
        yb = place("yb", [P, 4, T])
        evb = place("evb", [P, BANKS, T], offset=scratch)
        arena = at[0]
        actb = place("actb", [P, FT, 2 * T], F32R)
        arena_end = at[0]
        assert arena_end <= nc.sbuf_usable_end, (arena_end, nc.sbuf_usable_end)
        cur = [arena]

        def inside(name, shape, dt=F32):
            t = place(name, shape, dt, offset=cur[0])
            cur[0] = end_of(cur[0], shape)
            assert cur[0] <= arena_end, name
            return t

        z = inside("z", [P, ZT, T])
        nrm = place("nrm", [P, KT, T], offset=arena)
        c_sb = inside("c_sb", [P, C_N])
        wx_at = cur[0]
        wx = inside("wx", [P, KT, 32])
        wxlo = place("wxlo", [P, KT, 32], F32R, offset=wx_at)
        wxhi = inside("wxhi", [P, KT, 32], F32R)
        w2 = inside("w2", [P, 2, P])
        pos_sb = inside("pos_sb", [P, 2, CB])
        var = inside("var", [P, T])
        rstd = inside("rstd", [P, T])
        lg = inside("lg", [P, TB, 32])
        eg = inside("eg", [P, TB, 32])
        gate = inside("gate", [P, TB, 3 * NSA])
        lf = inside("lf", [P, TB, FOX])
        ln1 = inside("ln1", [P, TB, FOX])
        gel = inside("gel", [P, KV * NC])
        kcT = inside("kcT", [P, KV * NC])
        vc = inside("vc", [P, KV, P])
        vsw = inside("vsw", [P, 2, KV, TB, P])
        Lb = inside("Lb", [P, T])
        Rall = inside("Rall", [P, T])
        Rb = inside("Rb", [P, T])
        before = cur[0]
        xb = inside("xb", [P, 2, CB, KV * NC])
        rtmp = inside("rtmp", [P, NSA, T])
        cur[0] = before
        qf = inside("qf", [P, T])
        qn = inside("qn", [P, T])
        vfT = inside("vfT", [P, T])
        vf = inside("vf", [P, TB, P])
        pr = inside("pr", [P, 3, 3 * P])
        prc = inside("prc", [P, TB, P])
        pt = inside("pt", [P, 3, 3 * P])
        ptc = inside("ptc", [P, TB * P])
        sc = inside("sc", [P, TB, 16])
        mx = inside("mx", [P, 4, TB])
        nb = inside("nb", [P, 4, TB])
        rs = inside("rs", [P, 4, TB])
        rr = inside("rr", [P, 4, TB])

        ps = ctx.enter_context(nc.psum_tensor("ps", [P, 8, 512], F32))

        sem = {}

        def S(name):
            if name not in sem:
                sem[name] = ctx.enter_context(nc.semaphore(name))
            return sem[name]

        full = [S(f"slot_full{n}") for n in range(SLOTS)]
        ada_full = [S(f"ada_full{n}") for n in range(ASLOTS)]
        acol_ready, sq_added = S("acol_ready"), S("sq_added")
        x_loaded, par_loaded, ext_loaded = S("x_loaded"), S("par_loaded"), S("ext_loaded")
        stored = S("stored")
        w_used, w1_used, ada_used = S("w_used"), S("w1_used"), S("ada_used")
        hi_ready, lo_ready = S("hi_ready"), S("lo_ready")
        ada_sum, mod_ready = S("ada_sum"), S("mod_ready")
        bank_full, half_out, bank_free = S("bank_full"), S("half_out"), S("bank_free")
        conv_y, conv_done, silu_done, prod_done, acthi, act_ready = (
            S(n) for n in ("conv_y", "conv_done", "silu_done", "prod_done", "acthi", "act_ready"))
        sq_ready, ss_ready, ssb_ready, var_ready, root_ready, t_ready, hh_ready, h_ready = (
            S(n) for n in ("sq_ready", "ss_ready", "ssb_ready", "var_ready", "root_ready", "t_ready",
                           "hh_ready", "h_ready"))
        hhi_ready = S("hhi_ready")
        x_done, cact_ready, ones_ready = S("x_done"), S("cact_ready"), S("ones_ready")
        dve_own, act_own, pool_own = S("dve_own"), S("act_own"), S("pool_own")
        xsq_ready, xhi_ready, xlo_ready, ext_sum, lg_ready, eg_ready, lf_ready, cum_ready, bias_ready = (
            S(n) for n in ("xsq_ready", "xhi_ready", "xlo_ready", "ext_sum", "lg_ready", "eg_ready", "lf_ready",
                           "cum_ready", "bias_ready"))
        xb_ready, gel_ready, cmp_ready, cmpc_ready, vsw_t, vsw_ready = (
            S(n) for n in ("xb_ready", "gel_ready", "cmp_ready", "cmpc_ready",
                           "vsw_t", "vsw_ready"))
        zero_ready, stage_ready, r_ready, s_ready, vt_ready, vf_ready, nb_ready, p_ready, pn_ready = (
            S(n) for n in ("zero_ready", "stage_ready", "r_ready", "s_ready", "vt_ready", "vf_ready",
                           "nb_ready", "p_ready", "pn_ready"))
        pt_ready, ptc_ready, pv_ready, ohi_ready, o_done = (
            S(n) for n in ("pt_ready", "ptc_ready", "pv_ready", "ohi_ready", "o_done"))

        def modc(l, tile):
            return mod[:, l, tile:tile + 1]

        def flat(tile):
            return tile.rearrange("p o t -> p (o t)")

        def rows(w, k0, kn):
            return w[k0 * P:(k0 + kn) * P, :].rearrange("(k p) n -> p k n", p=P)

        def tiles_out(x, i=None):
            n = x.iters if i is None else i
            return n * (4 * x.groups) + (BANKS + 4 * x.g0)

        block = ctx.enter_context(nc.Block())

        @block.sync
        def _(sp):
            def slot_wait(s, i, x):
                if s < SLOTS:
                    return
                def need(s):
                    old = s - SLOTS
                    who, counts = {"M": (w_used, nm), "W": (w1_used, nw)}[kinds[old]]
                    return who, counts[old + 1]
                if isinstance(i, int):
                    sp.wait_ge(*need(s))
                else:
                    (who, c1), (_, c2) = need(s), need(s + x.r_per)
                    sp.wait_ge(who, (i - 1) * (c2 - c1) + c1)

            def source(x, i, item):
                kind, g, q = item
                l = x.layer
                if kind == "W":
                    w = (w_cmp1_k, w_cmp1_v)[q // 2][l]
                    return w[(q % 2) * 16 * P:(q % 2 + 1) * 16 * P, :].rearrange("(j p) n -> p j n", p=P)
                k0, kn = sum(x.ktiles[:q]), x.ktiles[q]
                if x.name == "fox":
                    return rows(w_in[l], k0, kn)[:, :, bass.ds(i * 512, 512)]
                if x.name == "nsa":
                    return rows(w_in[l], k0, kn)[:, :, bass.ds(i * 512 + (FF0 + FOX), 512)]
                if x.name == "out":
                    return rows(w_out[l], k0, kn)[:, :, bass.ds(i * 512, 512)]
                if x.name == "down":
                    return rows(w_down[l], k0, kn)[:, :, bass.ds(i * 512, 512)]
                return [rows(w_up[l], k0, kn)[:, :, bass.ds(i * 512 + (g * 256 + v * FF), 256)] for v in range(2)]

            def stream(x, i):
                for posn, item in enumerate(y for y in x.items if y[0] != "A"):
                    s = x.s0 + (i if isinstance(i, int) else 1) * x.r_per + posn
                    slot_wait(s, i, x)
                    slot = s % SLOTS
                    src = source(x, i, item)
                    if isinstance(src, list):
                        parts = [(raw[:, slot, :, v * 256:(v + 1) * 256], src[v]) for v in range(2)]
                    else:
                        n_rows = src.shape[1]
                        dst = raw[:, slot].rearrange("p k (j n) -> p (k j) n", n=P) if item[0] == "W" else raw[:, slot]
                        cut = (n_rows + 1) // 2
                        parts = [(dst[:, 0:cut], src[:, 0:cut]), (dst[:, cut:n_rows], src[:, cut:n_rows])]
                    for d_, s_ in parts:
                        sp.dma_start(d_, s_).then_inc(full[slot], 16)

            sp.dma_start(par_sb[:], par).then_inc(par_loaded, 16)
            sp.dma_start(x_sb[:], xT).then_inc(x_loaded, 16)
            for x in phases:
                if not x.r_per:
                    continue
                stream(x, 0)
                if x.name == "fox":
                    l = x.layer
                    if l:
                        sp.wait_ge(x_done, 2 * l)
                    sp.dma_start(c_sb[:], consts).then_inc(ext_loaded, 16)
                    sp.dma_start(w2[:, 0, :], w_cmp2_k[l]).then_inc(ext_loaded, 16)
                    sp.dma_start(w2[:, 1, :], w_cmp2_v[l]).then_inc(ext_loaded, 16)
                    sp.dma_start(pos_sb[:], pos[l]).then_inc(ext_loaded, 16)
                    sp.dma_start(wx[:, :, 0:FOX], rows(w_in[l], 0, KT)[:, :, FF0:FF0 + FOX]).then_inc(ext_loaded, 16)
                    sp.dma_start(wx[:, :, FOX:32], rows(w_in[l], 0, KT)[:, :, NG0:D_IN]).then_inc(ext_loaded, 16)
                repeat(sp, 1, x.iters, lambda i, x=x: stream(x, i))
            for q in range(4):
                sp.wait_ge(hh_ready, 4 * (2 * DEPTH) + q + 1)
                sp.dma_start(out[:, 4 * q:4 * q + 4, :], nrm[:, 4 * q:4 * q + 4, :]).then_inc(stored, 16)
            sp.wait_ge(stored, 64)

        EXT = 6 * 16

        def ring_pos(x, posn):
            return sum(y[0] != "A" for y in x.items[:posn])

        def arrived(eng, x, i, posn):
            per, n = x.r_per // SLOTS, ring_pos(x, posn)
            eng.wait_ge(full[n % SLOTS], i * (32 * per) + 32 * (x.s0 // SLOTS + n // SLOTS + 1))

        def m_index(x, i, posn):
            return i * x.m_per + (x.m0 + sum(y[0] == "M" for y in x.items[:posn]))

        def a_index(x, i, posn):
            return i * x.a_per + (x.a0 + sum(y[0] == "A" for y in x.items[:posn]))

        @block.tensor
        def _(pe):
            pe.wait_ge(ones_ready, 1)

            def main_step(x, i, posn):
                _, g, q = x.items[posn]
                m = m_index(x, i, posn)
                mi = ring_pos(x, posn)
                pe.wait_ge(lo_ready, m + 1)
                if x.name in ("fox", "up"):
                    pe.wait_ge(h_ready, 4 * (2 * x.layer + (x.name == "up")) + q + 1)
                if x.name == "down":
                    pe.wait_ge(act_ready, 1 + FT // 2 * x.layer + (sum(x.ktiles[:q + 1]) + 1) // 2)
                first, last = q == 0, q == len(x.ktiles) - 1
                k0, kn = sum(x.ktiles[:q]), x.ktiles[q]
                rhs = actb if x.name == "down" else hb
                for b in range(BANKS):
                    if first:
                        pe.wait_ge(bank_free, i * (4 * x.groups) + (4 * (x.g0 + g) + b + 1))
                    for k in range(kn):
                        w = slice(b * P, (b + 1) * P)
                        pe.matmul(ps[:, b, :], whi[:, mi % HSLOTS, k, w], rhs[:, k0 + k, :],
                                  start=first and k == 0, stop=False)
                        mm = pe.matmul(ps[:, b, T:2 * T], wlo[:, mi % SLOTS, k, w], rhs[:, k0 + k, 0:T],
                                       start=False, stop=last and k == kn - 1)
                    if last and b < BANKS - 1:
                        mm.then_inc(bank_full, 1)
                mm.then_inc(w_used, 1)

            def ada_total(x, i, posn):
                pe.wait_ge(ada_used, a_index(x, i, posn) + 1)
                for b in range(4):
                    mm = pe.matmul(ps[:, 4, b:b + 1], acc[:, b * P:(b + 1) * P], ones[:, 0:1], start=True, stop=True)
                mm.then_inc(ada_sum, 1)

            def run(x):
                def body(i):
                    for posn, item in enumerate(x.items):
                        if item[0] == "M":
                            main_step(x, i, posn)
                        elif item[0] == "A" and item[2] == KT - 1:
                            ada_total(x, i, posn)
                repeat(pe, 0, x.iters, body)

            def norm(n):
                if n:
                    pe.wait_ge(sq_added, BANKS + KT * n)
                else:
                    pe.wait_ge(ss_ready, 1)
                pe.matmul(ps[:, 5, 0:T], ones[:], ssum[:], start=True, stop=True).then_inc(ssb_ready, 1)

            ident = c_sb[:, C_ID:C_ID + P]
            neg = c_sb[:, C_NEG:C_NEG + P]

            def attention(l):
                pe.wait_ge(xlo_ready, l + 1)
                for tb in range(TB):
                    for k in range(KT):
                        hi = hb[:, k, tb * P:(tb + 1) * P]
                        lo = hb[:, k, T + tb * P:T + (tb + 1) * P]
                        dst = ps[:, 5, tb * 32:tb * 32 + 32]
                        pe.matmul(dst, hi, wxhi[:, k, :], start=k == 0, stop=False)
                        pe.matmul(dst, hi, wxlo[:, k, :], start=False, stop=False)
                        mm = pe.matmul(dst, lo, wxhi[:, k, :], start=False, stop=k == KT - 1)
                mm.then_inc(ext_sum, 1)
                pe.wait_ge(bank_free, tiles_out(phase("nsa", l)))
                for n, tile in enumerate((ZVS, ZVW)):
                    for g in range(KV):
                        for tb in range(TB):
                            dst = ps[:, 6 + n, (g * TB + tb) * P:(g * TB + tb + 1) * P]
                            mm = pe.transpose(dst, z[:, tile + g, tb * P:(tb + 1) * P], ident)
                mm.then_inc(vsw_t, 1)
                pe.wait_ge(lf_ready, l + 1)
                for tb in range(TB):
                    mm = pe.matmul(ps[0:FOX, 5, P:P + T], lf[:, tb, :], c_sb[:, C_TRI + tb * T:C_TRI + (tb + 1) * T],
                                   start=tb == 0, stop=tb == TB - 1)
                mm.then_inc(cum_ready, 1)
                x = phase("cmp", l)
                for kind in range(2):
                    pe.wait_ge(xb_ready, 2 * l + kind + 1)
                    for half in range(2):
                        arrived(pe, x, 0, 2 * kind + half)
                        for j in range(16):
                            w = raw[:, 2 * kind + half].rearrange("p k (j n) -> p (k j) n", n=P)[:, j, :]
                            mm = pe.matmul(ps[:, kind, 0:KV * NC], w, xb[:, kind, half * 16 + j, :],
                                           start=half == 0 and j == 0, stop=half == 1 and j == 15)
                        mm.then_inc(w1_used, 1)
                    pe.wait_ge(gel_ready, 2 * l + kind + 1)
                    if kind == 0:
                        mm = pe.matmul(ps[:, 2, 0:KV * NC], w2[:, 0, :], gel[:], start=True, stop=True)
                    else:
                        for g in range(KV):
                            mm = pe.matmul(ps[0:NC, 3, g * P:(g + 1) * P], gel[:, g * NC:(g + 1) * NC], w2[:, 1, :],
                                           start=True, stop=True)
                    mm.then_inc(cmp_ready, 1)
                pe.wait_ge(cmpc_ready, 2 * l + 2)
                pe.wait_ge(vsw_ready, l + 1)
                pe.wait_ge(zero_ready, l + 1)
                pe.wait_ge(bias_ready, l + 1)

                def head(h, kv):
                    pe.wait_ge(stage_ready, h + (l * FOX + 1))
                    pe.wait_ge(r_ready, h + (l * FOX + 1))

                    def scores(bank, q, keys, bias):
                        for n, (tb, kb) in enumerate(((0, 0), (1, 0), (1, 1))):
                            dst = ps[:, bank, n * P:(n + 1) * P]
                            diag = tb == kb
                            mm = pe.matmul(dst, q[:, tb * P:(tb + 1) * P], keys[:, kb * P:(kb + 1) * P],
                                           start=True, stop=not (bias or diag))
                            if bias:
                                mm = pe.matmul(dst, Lb[0:40, tb * P:(tb + 1) * P], Rb[0:40, kb * P:(kb + 1) * P],
                                               start=False, stop=not diag)
                            if diag:
                                mm = pe.matmul(dst, ident, neg, start=False, stop=True)
                        mm.then_inc(s_ready, 1)

                    scores(0, qf, flat(z[:, bass.ds(h + ZK, 1), :]), True)
                    for tb in range(TB):
                        mm = pe.matmul(ps[:, 3, tb * 16:tb * 16 + NC], qn[:, tb * P:(tb + 1) * P],
                                       kcT[:, kv * NC:(kv + 1) * NC], start=True, stop=True)
                    mm.then_inc(s_ready, 1)
                    scores(1, qn, z[:, ZKS + kv, :], False)
                    scores(2, qn, z[:, ZKW + kv, :], False)
                    for tb in range(TB):
                        mm = pe.transpose(ps[:, 6, T + tb * P:T + (tb + 1) * P], vfT[:, tb * P:(tb + 1) * P], ident)
                    mm.then_inc(vt_ready, 1)

                    def turn(u):
                        pe.wait_ge(pn_ready, h * 4 + (l * 4 * FOX + u + 1))
                        if u == 1:
                            src = [prc[:, 0, :], prc[:, 1, :]]
                        else:
                            src = [pr[:, u - (u > 0), n * P:(n + 1) * P] for n in range(3)]
                        for n, s in enumerate(src):
                            mm = pe.transpose(ps[:, 4 + u % 2, n * P:(n + 1) * P], s, ident)
                        mm.then_inc(pt_ready, 1)

                    def values(u):
                        pe.wait_ge(ptc_ready, h * 4 + (l * 4 * FOX + u + 1))
                        if u == 0:
                            pe.wait_ge(vf_ready, h + (l * FOX + 1))
                        if u <= 1:
                            pe.wait_ge(o_done, h * 2 + (l * 2 * FOX + u + 1))
                        if u == 1:
                            mm = pe.matmul(ps[:, 7, 0:T], vc[0:NC, kv, :], ptc[0:NC, :], start=True, stop=False)
                        else:
                            v = vf if u == 0 else vsw[:, u - 2, kv]
                            t = pt[:, u - (u > 0)]
                            if u == 0:
                                pe.matmul(ps[:, 6, 0:P], v[:, 0, :], t[:, 0:P], start=True, stop=True)
                                pe.matmul(ps[:, 6, P:T], v[:, 0, :], t[:, P:T], start=True, stop=False)
                                mm = pe.matmul(ps[:, 6, P:T], v[:, 1, :], t[:, T:3 * P], start=False, stop=True)
                            else:
                                pe.matmul(ps[:, 7, P:T], v[:, 1, :], t[:, T:3 * P], start=False, stop=False)
                                mm = pe.matmul(ps[:, 7, 0:T], v[:, 0, :], t[:, 0:T], start=False, stop=u == 3)
                        mm.then_inc(pv_ready, 1)

                    turn(0)
                    turn(1)
                    values(0)
                    turn(2)
                    values(1)
                    turn(3)
                    values(2)
                    values(3)

                for kv in range(KV):
                    repeat(pe, kv * GROUP, (kv + 1) * GROUP, lambda h, kv=kv: head(h, kv))

            for l in range(DEPTH):
                norm(2 * l)
                if l == 0:
                    run(phase("pre", 0))
                run(phase("fox", l))
                run(phase("nsa", l))
                run(phase("ext", l))
                attention(l)
                pe.wait_ge(o_done, 2 + 2 * FOX * (l + 1))
                run(phase("out", l))
                norm(2 * l + 1)
                run(phase("up", l))
                run(phase("down", l))
            norm(2 * DEPTH)

        @block.scalar
        def _(act):
            own = Chain(act, act_own)
            act.wait_ge(par_loaded, 16)
            act.activation(cact[:], par_sb[:, V_C:V_C + KT], ACT.Silu).then_inc(cact_ready, 1)

            def split_hi(x, i, posn):
                mi = ring_pos(x, posn)
                kn = x.ktiles[x.items[posn][2]]
                arrived(act, x, i, posn)
                if not (isinstance(i, int) and i == 0 and x.m0 + mi < HSLOTS):
                    act.wait_ge(w_used, i * x.m_per + (x.m0 + mi - HSLOTS + 1))
                act.activation(whi[:, mi % HSLOTS, 0:kn, :], raw[:, mi % SLOTS, 0:kn, :], ACT.Copy)\
                   .then_inc(hi_ready, 1)

            def full_bank(x, i, g, b):
                if b < BANKS - 1:
                    act.wait_ge(bank_full, i * (3 * x.groups) + (3 * (x.g0 + g) + b + 1))
                else:
                    act.wait_ge(w_used, i * x.m_per + (x.m0 + (g + 1) * (x.m_per // x.groups)))

            def out_plain(x, i, g, stage):
                if stage:
                    return
                for b in range(BANKS):
                    full_bank(x, i, g, b)
                    act.wait_ge(bank_free, i * (4 * x.groups) + (4 * (x.g0 + g) + b + 1))
                    if x.name in ("out", "down"):
                        act.wait_ge(sq_added, i * BANKS + (x.r0 + b + 1))
                    act.activation(evb[:, b, :], ps[:, b, T:2 * T], ACT.Copy).then_inc(half_out, 1)
                if x.name in ("out", "down"):
                    for b in range(BANKS):
                        act.wait_ge(bank_free, i * (4 * x.groups) + (4 * (x.g0 + g) + b + 1 + BANKS))
                        act.activation(evb[:, b, :], flat(x_sb[:, bass.ds(i * BANKS + b, 1), :]), ACT.Square)\
                           .then_inc(sq_ready, 1)

            def conv_col(l, tile, n):
                return par_sb[:, bass.ds(tile * 3 + (l * V_L + V_CW + n), 1)]

            def out_conv(x, i, g, stage):
                l = x.layer
                G = i * x.groups + g
                n0 = (x.layer) * (FT // 2)
                if stage == 0:
                    for b in range(BANKS):
                        full_bank(x, i, g, b)
                        act.wait_ge(conv_done, G * 1 + (n0 + 1))
                        act.activation(ub[:, b, 2:T + 2], ps[:, b, T:2 * T], ACT.Copy).then_inc(half_out, 1)
                elif stage == 1:
                    for b in range(BANKS):
                        tile = G * 2 + (b % 2 + (b // 2) * FT)
                        if b == 0:
                            act.wait_ge(act_ready, G + (n0 + 1))
                        act.wait_ge(bank_free, i * (4 * x.groups) + (BANKS + 4 * (x.g0 + g) + b + 1))
                        act.activation(yb[:, b, :], ub[:, b, 2:T + 2], ACT.Identity,
                                       bias=par_sb[:, bass.ds(tile + (l * V_L + V_CB), 1)],
                                       scale=conv_col(l, tile, 2)).then_inc(conv_y, 1)
                elif stage == 2:
                    act.wait_ge(conv_done, G * 1 + (n0 + 2))
                    act.activation(yb[:, 0:2, :], yb[:, 0:2, :], ACT.Silu).then_inc(silu_done, 1)
                else:
                    act.wait_ge(prod_done, G * 1 + (n0 + 1))
                    act.activation(actb[:, bass.ds(G * 2, 2), 0:T], yb[:, 0:2, :], ACT.Copy).then_inc(acthi, 1)

            def run(x):
                evac = out_conv if x.name == "up" else out_plain

                def body(i, first):
                    for posn, item in enumerate(x.items):
                        if item[0] == "M":
                            split_hi(x, i, posn)
                            _, g, q = item
                            if q < 4 and not (first and g == 0):
                                if g == 0:
                                    evac(x, i - 1, x.groups - 1, q)
                                else:
                                    evac(x, i, g - 1, q)
                if x.m_per:
                    body(0, True)
                    repeat(act, 1, x.iters, lambda i: body(i, False))
                    for stage in range(4):
                        evac(x, x.iters - 1, x.groups - 1, stage)

            def norm(n):
                final = n == 2 * DEPTH
                l = n // 2
                if n == 0:
                    act.wait_ge(x_loaded, 16)
                    act.activation(nrm[:], x_sb[:], ACT.Square).then_inc(xsq_ready, 1)
                act.wait_ge(var_ready, n + 1)
                act.activation(rstd[:], var[:], ACT.Sqrt).then_inc(root_ready, 1)
                shift = M_SHF if n % 2 else M_SHA
                if not final:
                    act.wait_ge(acol_ready, n + 1)
                for q in range(4):
                    act.wait_ge(t_ready, 4 * n + q + 1)
                    for k in range(4 * q, 4 * q + 4):
                        if final:
                            a = act.activation(nrm[:, k, :], nrm[:, k, :], ACT.Copy, scale=par_sb[:, V_FIN + k:V_FIN + k + 1])
                        else:
                            a = act.activation(nrm[:, k, :], nrm[:, k, :], ACT.Identity, bias=modc(l, shift + k),
                                               scale=acol[:, k:k + 1])
                    a.then_inc(hh_ready, 1)
                    if not final:
                        act.wait_ge(hh_ready, 4 * n + q + 1)
                        act.activation(hb[:, 4 * q:4 * q + 4, 0:T], nrm[:, 4 * q:4 * q + 4, :], ACT.Copy)\
                           .then_inc(hhi_ready, 1)

            def attention(l):
                act.wait_ge(ext_loaded, EXT * (l + 1))
                act.activation(wxhi[:], wx[:], ACT.Copy).then_inc(xhi_ready, 1)
                act.wait_ge(vsw_t, l + 1)
                for n in range(2):
                    a = act.activation(vsw[:, n].rearrange("p g t d -> p (g t d)"), ps[:, 6 + n, :], ACT.Copy)
                a.then_inc(vsw_ready, 1)
                act.wait_ge(lg_ready, l + 1)
                own(act.activation(ln1[:], lg[:, :, 0:FOX], ACT.Abs))
                own(act.activation(ln1[:], ln1[:], ACT.Exp, scale=-1.0))
                act.activation(eg[:, :, FOX:32], lg[:, :, FOX:32], ACT.Exp, scale=-1.0)
                act.activation(ln1[:], ln1[:], ACT.Ln, bias=1.0).then_inc(eg_ready, 1)
                for kind in range(2):
                    act.wait_ge(w1_used, 4 * l + 2 * kind + 2)
                    act.activation(gel[:], ps[:, kind, 0:KV * NC], ACT.Gelu_apprx_tanh).then_inc(gel_ready, 1)

                def head(h):
                    def expo(u):
                        act.wait_ge(nb_ready, h * 4 + (l * 4 * FOX + u + 1))
                        if u == 1:
                            a = act.activation(sc[:, :, 0:NC], sc[:, :, 0:NC], ACT.Exp, scale=SCALE)
                        else:
                            n = u - (u > 0)
                            bank = (0, 3, 1, 2)[u]
                            act.activation(pr[:, n, 0:P], ps[:, bank, 0:P], ACT.Exp, bias=nb[:, u, 0:1],
                                           scale=SCALE, accum_out=rs[:, u, 0:1])
                            a = act.activation(pr[:, n, P:3 * P], ps[:, bank, P:3 * P], ACT.Exp, bias=nb[:, u, 1:2],
                                               scale=SCALE, accum_out=rs[:, u, 1:2])
                        a.then_inc(p_ready, 1)

                    def copy(u):
                        act.wait_ge(pt_ready, h * 4 + (l * 4 * FOX + u + 1))
                        if u == 1:
                            a = act.activation(ptc[:], ps[:, 5, 0:TB * P], ACT.Copy)
                        else:
                            a = act.activation(pt[:, u - (u > 0), :], ps[:, 4 + u % 2, 0:3 * P], ACT.Copy)
                        a.then_inc(ptc_ready, 1)

                    def high(n):
                        act.wait_ge(pv_ready, h * 4 + (l * 4 * FOX + (1 if n == 0 else 4)))
                        act.activation(flat(hb[:, bass.ds(h + n * FOX, 1), 0:T]), ps[:, 6 + n, 0:T], ACT.Copy)\
                           .then_inc(ohi_ready, 1)

                    act.wait_ge(vt_ready, h + (l * FOX + 1))
                    act.activation(vf[:].rearrange("p t d -> p (t d)"), ps[:, 6, T:2 * T], ACT.Copy).then_inc(vf_ready, 1)
                    expo(0)
                    expo(1)
                    copy(0)
                    expo(2)
                    copy(1)
                    expo(3)
                    copy(2)
                    high(0)
                    copy(3)
                    high(1)

                repeat(act, 0, FOX, head)

            for l in range(DEPTH):
                norm(2 * l)
                run(phase("fox", l))
                run(phase("nsa", l))
                attention(l)
                run(phase("out", l))
                norm(2 * l + 1)
                run(phase("up", l))
                run(phase("down", l))
            norm(2 * DEPTH)

        @block.vector
        def _(dve):
            own = Chain(dve, dve_own)
            dve.sem_inc(bank_free, BANKS)
            dve.sem_inc(conv_done, 1)
            dve.sem_inc(o_done, 2)
            dve.sem_inc(sq_added, BANKS)
            dve.sem_inc(act_ready, 1)
            dve.memset(ones[:], 1.0).then_inc(ones_ready, 1)
            dve.wait_ge(cact_ready, 1)

            def split_lo(x, i, posn):
                kn = x.ktiles[x.items[posn][2]]
                mi = ring_pos(x, posn)
                slot = mi % SLOTS
                dve.wait_ge(hi_ready, m_index(x, i, posn) + 1)
                dve.tensor_tensor(wlo[:, slot, 0:kn, :], raw[:, slot, 0:kn, :],
                                  whi[:, mi % HSLOTS, 0:kn, :].bitcast(F32), ALU.subtract).then_inc(lo_ready, 1)

            def ada_step(x, i, posn):
                kt = x.items[posn][2]
                n = sum(y[0] == "A" for y in x.items[:posn])
                slot = n % ASLOTS
                per = x.a_per // ASLOTS
                dve.wait_ge(ada_full[slot], i * (16 * per) + 16 * (x.a0 // ASLOTS + n // ASLOTS + 1))
                c = cact[:, kt:kt + 1]
                if kt == 0:
                    a = dve.tensor_scalar(acc[:], ada_raw[:, slot, :], c, None, ALU.mult)
                else:
                    dve.wait_ge(ada_used, a_index(x, i, posn))
                    a = dve.scalar_tensor_tensor(out=acc[:], in0=ada_raw[:, slot, :], scalar=c, in1=acc[:],
                                                 op0=ALU.mult, op1=ALU.add)
                a.then_inc(ada_used, 1)

            def ada_out(x, i, c):
                first = x.first_chunk + c
                l = first // CHUNKS
                dve.wait_ge(ada_sum, i * x.chunks + (first + 1))
                col = i * (4 * x.chunks) + (first % CHUNKS) * 4
                own(dve.tensor_tensor(mod[:, l, bass.ds(col, 4)], ps[:, 4, 0:4],
                                      par_sb[:, bass.ds(col + (l * V_L + V_BA), 4)], ALU.add))

            def out_plain(x, i, g, stage):
                if stage:
                    return
                l = x.layer
                for b in range(BANKS):
                    n = i * (4 * x.groups) + (4 * (x.g0 + g) + b + 1)
                    dve.wait_ge(half_out, n)
                    tile = i * 4 + b
                    if x.name in ("fox", "nsa"):
                        at_ = tile + (ZNQ if x.name == "nsa" else 0)
                        dve.tensor_tensor(flat(z[:, bass.ds(at_, 1), :]), ps[:, b, 0:T], evb[:, b, :], ALU.add)\
                           .then_inc(bank_free, 1)
                    else:
                        own(dve.tensor_tensor(evb[:, b, :], ps[:, b, 0:T], evb[:, b, :], ALU.add))
                        gate_ = mod[:, l, bass.ds(tile + (M_GA if x.name == "out" else M_GF), 1)]
                        xt = flat(x_sb[:, bass.ds(tile, 1), :])
                        dve.scalar_tensor_tensor(out=xt, in0=evb[:, b, :], scalar=gate_, in1=xt,
                                                 op0=ALU.mult, op1=ALU.add).then_inc(bank_free, 1)
                if x.name in ("out", "down"):
                    for b in range(BANKS):
                        n = i * BANKS + (x.r0 + b + 1)
                        dve.wait_ge(sq_ready, n)
                        dve.wait_ge(sq_added, n + (BANKS - 1))
                        dve.tensor_tensor(ssum[:], ssum[:], evb[:, b, :], ALU.add).then_inc(sq_added, 1)

            def conv_col(l, tile, n):
                return par_sb[:, bass.ds(tile * 3 + (l * V_L + V_CW + n), 1)]

            def out_conv(x, i, g, stage):
                l = x.layer
                G = i * x.groups + g
                n0 = l * (FT // 2)
                if stage == 0:
                    for b in range(BANKS):
                        n = i * (4 * x.groups) + (4 * (x.g0 + g) + b + 1)
                        dve.wait_ge(half_out, n)
                        u = ub[:, b, 2:T + 2]
                        dve.tensor_tensor(u, ps[:, b, 0:T], u, ALU.add).then_inc(bank_free, 1)
                elif stage == 1:
                    for tap in (1, 0):
                        for b in range(BANKS):
                            tile = G * 2 + (b % 2 + (b // 2) * FT)
                            if tap == 1:
                                dve.wait_ge(conv_y, G * 4 + (4 * n0 + b + 1))
                            a = dve.scalar_tensor_tensor(out=yb[:, b, :], in0=ub[:, b, tap:T + tap],
                                                         scalar=conv_col(l, tile, tap), in1=yb[:, b, :],
                                                         op0=ALU.mult, op1=ALU.add)
                            if tap == 1:
                                if b == BANKS - 1:
                                    own(a)
                            elif b == BANKS - 1:
                                a.then_inc(conv_done, 1)
                elif stage == 2:
                    dve.wait_ge(silu_done, G * 1 + (n0 + 1))
                    dve.tensor_tensor(yb[:, 0:2, :], yb[:, 0:2, :], yb[:, 2:4, :], ALU.mult).then_inc(prod_done, 1)
                else:
                    dve.wait_ge(acthi, G * 1 + (n0 + 1))
                    hi = actb[:, bass.ds(G * 2, 2), 0:T]
                    dve.tensor_tensor(actb[:, bass.ds(G * 2, 2), T:2 * T], yb[:, 0:2, :], hi.bitcast(F32), ALU.subtract)\
                       .then_inc(act_ready, 1)

            def run(x):
                evac = out_conv if x.name == "up" else out_plain
                if not x.m_per:
                    def only(i):
                        for posn, item in enumerate(x.items):
                            if item[0] == "A":
                                ada_step(x, i, posn)
                                if item[2] == KT - 1:
                                    ada_out(x, i, item[1])
                    if x.a_per:
                        own.loop(0, x.iters, x.chunks, only)
                    return
                per = x.chunks
                if x.name in ("out", "down"):
                    per += 4
                    own(dve.memset(ssum[:], 0.0))
                if x.name == "up":
                    per += x.groups

                def body(i, first):
                    pending = None if first or not x.chunks else (i - 1, x.chunks - 1)
                    for posn, item in enumerate(x.items):
                        if item[0] == "M":
                            split_lo(x, i, posn)
                            _, g, q = item
                            if q < 4 and not (first and g == 0):
                                if g == 0:
                                    evac(x, i - 1, x.groups - 1, q)
                                else:
                                    evac(x, i, g - 1, q)
                            if pending:
                                ada_out(x, *pending)
                                pending = None
                        else:
                            ada_step(x, i, posn)
                            if item[2] == KT - 1:
                                pending = (i, item[1])
                    assert pending is None or pending[1] == x.chunks - 1

                body(0, True)
                own.loop(1, x.iters, per, lambda i: body(i, False))
                for stage in range(4):
                    evac(x, x.iters - 1, x.groups - 1, stage)
                if x.chunks:
                    ada_out(x, x.iters - 1, x.chunks - 1)

            def norm(n):
                final = n == 2 * DEPTH
                if n == 0:
                    dve.wait_ge(xsq_ready, 1)
                    dve.tensor_reduce(ssum[:], nrm[:].rearrange("p k t -> p t k"), AX.X, ALU.add).then_inc(ss_ready, 1)
                else:
                    column_scale(n)
                dve.wait_ge(ssb_ready, n + 1)
                dve.tensor_scalar(var[:], ps[:, 5, 0:T], 1.0 / D, EPS, ALU.mult, ALU.add).then_inc(var_ready, 1)
                dve.wait_ge(root_ready, n + 1)
                own(dve.reciprocal(rstd[:], rstd[:]))
                for q in range(4):
                    dve.tensor_tensor(nrm[:, 4 * q:4 * q + 4, :], x_sb[:, 4 * q:4 * q + 4, :],
                                      rstd[:].unsqueeze(1).broadcast_to([P, 4, T]), ALU.mult).then_inc(t_ready, 1)
                    if n and not final and q:
                        low(n, q - 1)
                if n == 0:
                    run(phase("pre", 0))
                    column_scale(0)
                    for q in range(3):
                        low(n, q)
                if not final:
                    low(n, 3)

            def column_scale(n):
                if n == 2 * DEPTH:
                    return
                l = n // 2
                gain = V_GF if n % 2 else V_GA
                scl = M_SCF if n % 2 else M_SCA
                dve.scalar_tensor_tensor(out=acol[:], in0=mod[:, l, scl:scl + KT], scalar=1.0,
                                         in1=par_sb[:, l * V_L + gain:l * V_L + gain + KT],
                                         op0=ALU.add, op1=ALU.mult).then_inc(acol_ready, 1)

            def low(n, q):
                dve.wait_ge(hhi_ready, 4 * n + q + 1)
                hi = hb[:, 4 * q:4 * q + 4, 0:T].bitcast(F32)
                dve.tensor_tensor(hb[:, 4 * q:4 * q + 4, T:2 * T], nrm[:, 4 * q:4 * q + 4, :], hi, ALU.subtract)\
                   .then_inc(h_ready, 1)

            def rope(t0, n):
                zz = z[:, t0:t0 + n, :]
                half = HD // 2
                for a, b in ((0, half), (half, 0)):
                    sin = c_sb[b:b + half, C_SIN:C_SIN + T].unsqueeze(1).broadcast_to([half, n, T])
                    last = dve.tensor_tensor(rtmp[a:a + half, 0:n, :], z[b:b + half, t0:t0 + n, :], sin, ALU.mult)
                    own(last)
                cos = c_sb[:, C_COS:C_COS + T].unsqueeze(1).broadcast_to([P, n, T])
                own(dve.tensor_tensor(zz, zz, cos, ALU.mult))
                own(dve.tensor_tensor(zz, zz, rtmp[:, 0:n, :], ALU.add))

            def blocks(kind, l):
                for g in range(KV):
                    tile = z[:, (ZVC if kind else ZKC) + g, :]
                    for half in range(2):
                        src = tile[:, half * 16:half * 16 + NC * CS].rearrange("p (n j) -> p j n", j=CS)
                        ps_ = pos_sb[:, kind, half * 16:half * 16 + 16].unsqueeze(2).broadcast_to([P, 16, NC])
                        a = dve.tensor_tensor(xb[:, kind, half * 16:half * 16 + 16, g * NC:(g + 1) * NC], src, ps_, ALU.add)
                a.then_inc(xb_ready, 1)

            def attention(l):
                dve.wait_ge(xhi_ready, l + 1)
                dve.tensor_tensor(wxlo[:], wx[:], wxhi[:].bitcast(F32), ALU.subtract).then_inc(xlo_ready, 1)
                dve.wait_ge(bank_free, tiles_out(phase("nsa", l)))
                blocks(1, l)
                dve.wait_ge(ext_sum, l + 1)
                e = ps[:, 5, 0:64].rearrange("p (t n) -> p t n", t=TB)
                bf = par_sb[:, l * V_L + V_BF:l * V_L + V_BF + FOX].unsqueeze(1).broadcast_to([P, TB, FOX])
                dve.tensor_tensor(lg[:, :, 0:FOX], e[:, :, 0:FOX], bf, ALU.add)
                dve.tensor_scalar(lg[:, :, FOX:32], e[:, :, FOX:32], 1.0, None, ALU.mult).then_inc(lg_ready, 1)
                rope(ZKC, KV)
                blocks(0, l)
                dve.wait_ge(eg_ready, l + 1)
                own(dve.tensor_scalar(gate[:], eg[:, :, FOX:32], 1.0, None, ALU.add))
                own(dve.reciprocal(gate[:], gate[:]))
                own(dve.tensor_scalar(lf[:], lg[:, :, 0:FOX], 0.0, ROOT, ALU.min, ALU.mult))
                dve.scalar_tensor_tensor(out=lf[:], in0=ln1[:], scalar=-ROOT, in1=lf[:], op0=ALU.mult, op1=ALU.add)\
                   .then_inc(lf_ready, 1)
                rope(ZKS, KV)
                rope(ZKW, KV)
                rope(ZNQ, NSA)
                dve.wait_ge(cum_ready, l + 1)
                dve.wait_ge(zero_ready, l + 1)
                cum = ps[0:FOX, 5, P:P + T]
                own(dve.tensor_scalar(Rall[0:FOX, :], cum, -1.0, None, ALU.mult))
                dve.tensor_scalar(Lb[32:32 + FOX, :], cum, 1.0, None, ALU.mult).then_inc(bias_ready, 1)
                dve.wait_ge(cmp_ready, 2 * l + 1)
                dve.tensor_copy(kcT[:], ps[:, 2, 0:KV * NC]).then_inc(cmpc_ready, 1)
                dve.wait_ge(cmp_ready, 2 * l + 2)
                dve.tensor_copy(vc[0:NC].rearrange("p g d -> p (g d)"), ps[0:NC, 3, 0:KV * P]).then_inc(cmpc_ready, 1)

                cneg = c_sb[:, C_CNEG:C_CNEG + 32].rearrange("p (t n) -> p t n", t=TB)[:, :, 0:NC]
                c01 = c_sb[:, C_C01:C_C01 + 32].rearrange("p (t n) -> p t n", t=TB)[:, :, 0:NC]

                def head(h):
                    dve.tensor_scalar(Rb[0:40, :], Rall[0:40, :], c_sb[0:40, bass.ds(h + C_SEL, 1)], None, ALU.mult)\
                       .then_inc(r_ready, 1)

                    def top(u):
                        dve.wait_ge(s_ready, h * 4 + (l * 4 * FOX + u + 1))
                        bank = (0, 3, 1, 2)[u]
                        if u == 1:
                            s = ps[:, bank, 0:32].rearrange("p (t n) -> p t n", t=TB)[:, :, 0:NC]
                            own(dve.tensor_tensor(sc[:, :, 0:NC], s, cneg, ALU.add))
                            own(dve.tensor_reduce(mx[:, u, :], sc[:, :, 0:NC], AX.X, ALU.max))
                            for tb in range(TB):
                                a = dve.tensor_scalar(sc[:, tb, 0:NC], sc[:, tb, 0:NC], mx[:, u, tb:tb + 1], None, ALU.subtract)
                            a.then_inc(nb_ready, 1)
                        else:
                            dve.tensor_reduce(mx[:, u, 0:1], ps[:, bank, 0:P], AX.X, ALU.max)
                            own(dve.tensor_reduce(mx[:, u, 1:2], ps[:, bank, P:3 * P], AX.X, ALU.max))
                            dve.tensor_scalar(nb[:, u, :], mx[:, u, :], -SCALE, None, ALU.mult).then_inc(nb_ready, 1)

                    def scale(u):
                        dve.wait_ge(p_ready, h * 4 + (l * 4 * FOX + u + 1))
                        if u == 1:
                            own(dve.tensor_tensor(sc[:, :, 0:NC], sc[:, :, 0:NC], c01, ALU.mult))
                            own(dve.tensor_reduce(rs[:, u, :], sc[:, :, 0:NC], AX.X, ALU.add))
                        own(dve.tensor_scalar(rr[:, u, :], rs[:, u, :], TINY, None, ALU.max))
                        own(dve.reciprocal(rr[:, u, :], rr[:, u, :]))
                        if u:
                            g = gate[:, :, bass.ds(h * 3 + (u - 1), 1)].rearrange("p t n -> p (t n)")
                            own(dve.tensor_tensor(rr[:, u, :], rr[:, u, :], g, ALU.mult))
                        for tb in range(TB):
                            r = rr[:, u, tb:tb + 1]
                            if u == 1:
                                a = dve.tensor_scalar(prc[:, tb, 0:NC], sc[:, tb, 0:NC], r, None, ALU.mult)
                            else:
                                cols = pr[:, u - (u > 0), 0:P] if tb == 0 else pr[:, u - (u > 0), P:3 * P]
                                a = dve.tensor_scalar(cols, cols, r, None, ALU.mult)
                        a.then_inc(pn_ready, 1)

                    def low_(n):
                        dve.wait_ge(ohi_ready, h * 2 + (l * 2 * FOX + n + 1))
                        tile = bass.ds(h + n * FOX, 1)
                        dve.tensor_tensor(flat(hb[:, tile, T:2 * T]), ps[:, 6 + n, 0:T], flat(hb[:, tile, 0:T]).bitcast(F32),
                                          ALU.subtract).then_inc(o_done, 1)

                    top(0)
                    top(1)
                    scale(0)
                    top(2)
                    scale(1)
                    top(3)
                    scale(2)
                    scale(3)
                    low_(0)
                    low_(1)

                own.loop(0, FOX, 18, head)

            for l in range(DEPTH):
                norm(2 * l)
                run(phase("fox", l))
                run(phase("nsa", l))
                run(phase("ext", l))
                attention(l)
                run(phase("out", l))
                dve.wait_ge(bank_free, tiles_out(phase("out", l)))
                dve.sem_inc(x_done, 1)
                norm(2 * l + 1)
                own(dve.memset(ub[:, :, 0:2], 0.0))
                run(phase("up", l))
                run(phase("down", l))
                dve.wait_ge(bank_free, tiles_out(phase("down", l)))
                dve.sem_inc(x_done, 1)
            norm(2 * DEPTH)

        @block.gpsimd
        def _(pool):
            own = Chain(pool, pool_own)

            def load_ada(x):
                def one(i, n):
                    c = x.first_chunk + n // KT
                    lc = c // CHUNKS
                    assert (c + (x.iters - 1) * x.chunks) // CHUNKS == lc
                    if not (isinstance(i, int) and x.a0 + i * x.a_per + n < ASLOTS):
                        pool.wait_ge(ada_used, i * x.a_per + (x.a0 + n - ASLOTS + 1))
                    k = n % KT
                    pool.dma_start(ada_raw[:, n % ASLOTS, :],
                                   w_ada[lc, k * P:(k + 1) * P, bass.ds(i * (512 * x.chunks) + (c % CHUNKS) * 512, 512)])\
                        .then_inc(ada_full[n % ASLOTS], 16)

                def body(i):
                    for n in range(x.a_per):
                        one(i, n)
                if x.a_per:
                    body(0)
                    repeat(pool, 1, x.iters, body)

            def loads(l, *names):
                for name in names:
                    load_ada(phase(name, l))

            loads(0, "pre")
            for l in range(DEPTH):
                loads(l, "fox", "nsa", "ext")
                pool.wait_ge(bank_free, tiles_out(phase("nsa", l)))
                own(pool.memset(Lb[:], 0.0))
                own(pool.memset(Rall[:], 0.0))
                pool.memset(Lb[0:FOX, :], 1.0)
                pool.memset(Rall[32:32 + FOX, :], 1.0).then_inc(zero_ready, 1)

                def stage(h):
                    pool.tensor_copy(qf[:], flat(z[:, bass.ds(h + ZQ, 1), :]))
                    pool.tensor_copy(vfT[:], flat(z[:, bass.ds(h + ZV, 1), :]))
                    pool.tensor_copy(qn[:], flat(z[:, bass.ds(h + ZNQ, 1), :])).then_inc(stage_ready, 1)

                pool.wait_ge(bias_ready, l + 1)
                pool.wait_ge(cmp_ready, 2 * l + 2)
                own(pool.memset(prc[:], 0.0))
                stage(0)

                def following(h):
                    pool.wait_ge(vt_ready, h + (l * FOX + 1))
                    stage(h + 1)

                repeat(pool, 0, FOX - 1, following)
                loads(l, "out", "up", "down")


_OUT = (P, KT, T)


def kernel(**inputs):
    import numpy as _np
    import concourse.bacc as _bacc
    from concourse import mybir as _mybir
    from concourse.bass_utils import run_bass_kernel_spmd as _run

    g = {k: _np.asarray(v) for k, v in inputs.items()}

    def cols(a, *tail):
        a = a.reshape((a.shape[0], -1, P) + tail)
        return _np.moveaxis(a, 2, 0)

    def per_layer(a):
        return a.reshape(P, DEPTH, -1)

    par = _np.concatenate([
        per_layer(cols(g["attn_norm_g"])),
        per_layer(cols(g["ffn_norm_g"])),
        per_layer(cols(g["b_ada"])),
        per_layer(cols(_np.ascontiguousarray(_np.moveaxis(g["conv_w"], 1, 2)), 3)),
        per_layer(cols(g["conv_b"])),
        _np.broadcast_to(g["b_fgate"][None], (P, DEPTH, FOX)),
    ], axis=2).reshape(P, -1)
    par = _np.concatenate([par, g["final_norm_g"].reshape(KT, P).T, g["c"].reshape(KT, P).T], axis=1)
    pos = _np.stack([g["cmp_pos_k"], g["cmp_pos_v"]], axis=1).transpose(0, 3, 1, 2)
    arrays = {
        "xT": g["x"][0].T.reshape(KT, P, T).transpose(1, 0, 2),
        "par": par,
        "pos": pos,
        "consts": constants(),
    }
    for name in ("w_ada", "w_in", "w_cmp1_k", "w_cmp1_v", "w_cmp2_k", "w_cmp2_v", "w_out", "w_up", "w_down"):
        arrays[name] = g[name]
    arrays = {f"in_{k}": _np.ascontiguousarray(v) for k, v in arrays.items()}
    nc = _bacc.Bacc("TRN2", target_bir_lowering=False, num_devices=1)
    args = [nc.dram_tensor(k, v.shape, _mybir.dt.from_np(v.dtype), kind="ExternalInput").ap()
            for k, v in arrays.items()]
    args.append(nc.dram_tensor("out_T", _OUT, _mybir.dt.float32, kind="ExternalOutput").ap())
    trunk(nc, *args)
    r = _run(nc, [arrays], core_ids=[0])
    got = r.results[0]["out_T"]
    return _np.ascontiguousarray(got.transpose(2, 1, 0).reshape(1, T, D))
```

```python
from contextlib import ExitStack

import numpy as np
import concourse.bass as bass
from concourse import mybir

ALU = mybir.AluOpType
ACT = mybir.ActivationFunctionType
AX = mybir.AxisListType
F32 = mybir.dt.float32
F32R = mybir.dt.float32r

P = 128
D = 2048
T = 256
TB = T // P
KT = D // P
DEPTH = 2
HD = 128
FOX = 8
NSA = 8
KV = 2
GROUP = NSA // KV
FF = 5632
FT = FF // P
D_IN = 3 * FOX * HD + FOX + NSA * HD + 6 * KV * HD + 3 * NSA
NG0 = D_IN - 3 * NSA
FF0 = 3 * FOX * HD
CB, CS = 32, 16
NC = (T - CB) // CS + 1
SCALE = 1.0 / float(np.sqrt(HD))
ROOT = float(np.sqrt(HD))
EPS = 1e-6
NEG = -1e30
TINY = 1e-30

ZQ, ZK, ZV = 0, FOX, 2 * FOX
ZNQ = 3 * FOX
ZKC, ZVC, ZKS, ZVS, ZKW, ZVW = (ZNQ + NSA + KV * n for n in range(6))
ZT = ZNQ + NSA + 6 * KV

SLOTS = 4
ASLOTS = 4
HSLOTS = 2
BANKS = 4
CHUNKS = 6 * D // 512

PRE_CUTS = (1, 2, 3)
LEAD = 2
HIDDEN = (2, 4, 6, 7)

V_GA, V_GF = 0, KT
V_CW = 2 * KT
V_CB = V_CW + 2 * FT * 3
V_BF = V_CB + 2 * FT
V_L = V_BF + FOX
V_FIN = DEPTH * V_L
V_C = V_FIN + KT
V_BA = V_C + KT
V_N = V_BA + DEPTH * 6 * KT
M_SHA, M_SCA, M_GA, M_SHF, M_SCF, M_GF = (KT * n for n in range(6))

C_ID = 0
C_NEG = C_ID + P
C_TRI = C_NEG + P
C_COS = C_TRI + TB * T
C_SIN = C_COS + T
C_CNEG = C_SIN + T
C_C01 = C_CNEG + TB * 16
C_SEL = C_C01 + TB * 16
C_N = C_SEL + FOX


def constants():
    c = np.zeros((P, C_N), np.float32)
    p = np.arange(P)
    t = np.arange(T)
    c[:, C_ID:C_ID + P] = np.eye(P)
    c[:, C_NEG:C_NEG + P] = np.where(p[None, :] <= p[:, None], 0.0, NEG)
    for b in range(TB):
        c[:, C_TRI + b * T:C_TRI + (b + 1) * T] = t[None, :] >= b * P + p[:, None]
        seen = np.arange(NC)[None, :] * CS + CB - 1 <= (b * P + p)[:, None]
        c[:, C_CNEG + b * 16:C_CNEG + b * 16 + NC] = np.where(seen, 0.0, NEG)
        c[:, C_C01 + b * 16:C_C01 + b * 16 + NC] = seen
    half = HD // 2
    inv = np.float32(10000.0) ** (-np.arange(0, HD, 2, dtype=np.float32) / np.float32(HD))
    ang = (t.astype(np.float32)[:, None] * inv[None, :]).astype(np.float32).T
    c[:, C_COS:C_COS + T] = np.concatenate([np.cos(ang), np.cos(ang)])
    c[:half, C_SIN:C_SIN + T] = np.sin(ang)
    c[half:, C_SIN:C_SIN + T] = -np.sin(ang)
    for h in range(FOX):
        c[h, C_SEL + h] = 1.0
        c[32 + h, C_SEL + h] = 1.0
    return c


def tiles_of_ada(items):
    return sum({"A": 1, "P": 3}.get(x[0], 0) for x in items)


class Phase:

    def __init__(self, name, layer, iters, items, groups=0, ktiles=(), first_group=0, after=None, first_chunk=0):
        self.name, self.layer, self.iters, self.items = name, layer, iters, items
        self.groups, self.ktiles, self.first_group = groups, ktiles, first_group
        self.first_chunk = first_chunk
        self.after, self.hands_on = after, False
        if after:
            after.hands_on = True
        self.m_per = sum(x[0] == "M" for x in items)
        self.b_per = sum(x[0] == "A" for x in items)
        self.r_per = len(items) - self.b_per
        self.a_per = tiles_of_ada(items)
        self.chunks = self.b_per // KT + sum(x[0] == "P" for x in items) // (KT // 4)


def weave(groups, steps, adas=()):
    out, a = [], 0
    for n in range(groups * steps):
        out.append(("M", n // steps, n % steps))
        for _ in range(adas[n % len(adas)] if adas else 0):
            out.append(("A", a // KT, a % KT))
            a += 1
    return out


def plan():
    four = (4, 4, 4, 4)
    down = (4,) * 8 + (3,) * 4
    one = (4,)
    heads = (3, 5, 3, 5)
    half = (2,)
    ph, chunk = [], 0

    def add(name, layer, iters, items, **k):
        nonlocal chunk
        x = Phase(name, layer, iters, items, first_chunk=chunk, **k)
        chunk += x.chunks * iters
        ph.append(x)
        return x

    for l in range(DEPTH):
        if l == 0:
            add("pre", l, 4, [("P", c, r) for c in range(2) for r in range(KT // 4)])
        nsaa = add("nsaa", l, 3, weave(1, 4, () if l else one), groups=1, ktiles=four)
        items = weave(2, 4, () if l else one)
        for n in range(3, -1, -1):
            s = HIDDEN[n]
            at = items.index(("M", s // 4, s % 4)) + 1
            items.insert(at, ("W", 0, n))
        nsab = add("nsab", l, 1, items, groups=2, ktiles=four, first_group=3, after=nsaa)
        foxa = add("foxa", l, 1, weave(2, 4, half if l else one), groups=2, ktiles=four, after=nsab)
        add("foxb", l, 4, weave(1, 4, heads), groups=1, ktiles=four, first_group=2, after=foxa)
        add("outn", l, 2, weave(2, 2), groups=2, ktiles=(4, 4))
        add("outf", l, 1, weave(4, 2, () if l else (2,)), groups=4, ktiles=(4, 4))
        up = add("up", l, 11, weave(2, 4, () if l else (3, 0, 2, 3, 3, 0, 3, 2)), groups=2, ktiles=four)
        adas = (0, 1, 1, 2, 1, 2, 2, 2, 2, 2, 1, 0) if l else (2, 2, 3, 3, 3, 3, 2, 3, 3, 3, 3, 2)
        add("down", l, 4, weave(1, 12, adas), groups=1, ktiles=down, after=up)
    assert chunk == DEPTH * CHUNKS
    s = m = a = b = g = r = 0
    kinds = []
    for x in ph:
        x.s0, x.m0, x.a0, x.b0, x.g0, x.r0 = s, m, a, b, g, r
        assert s % SLOTS == 0 and x.r_per % SLOTS == 0 and x.b_per % ASLOTS == 0
        assert m % HSLOTS == 0 and x.m_per % HSLOTS == 0
        kinds += [y[0] for y in x.items if y[0] != "A"] * x.iters
        s += x.r_per * x.iters
        r += BANKS * x.iters * x.groups * (x.name in ("outf", "down"))
        m += x.m_per * x.iters
        a += x.a_per * x.iters
        b += x.b_per * x.iters
        g += x.groups * x.iters
    return ph, kinds


def repeat(eng, start, end, body):
    if end - start == 1:
        body(start)
    elif end > start:
        with eng.Fori(start, end) as i:
            body(i)


class Chain:

    def __init__(self, eng, sem):
        self.eng, self.sem, self.base, self.k, self.i, self.per = eng, sem, 0, 0, None, 0

    def __call__(self, ins):
        ins.then_inc(self.sem, 1)
        self.k += 1
        at = self.base + self.k if self.i is None else self.i * self.per + (self.base + self.k)
        self.eng.wait_ge(self.sem, at)

    def loop(self, start, end, per, body):
        self.base, self.k = self.base + self.k, 0

        def one(i):
            self.i, self.per, self.k = i, per, 0
            self.base -= start * per
            body(i)
            self.base += start * per
            assert self.k == per, (self.k, per)

        repeat(self.eng, start, end, one)
        self.i, self.k = None, 0
        self.base += per * (end - start)


def trunk(nc, xT, par, pos, consts, w_ada, w_in, w_cmp1_k, w_cmp1_v, w_cmp2_k, w_cmp2_v,
          w_out, w_up, w_down, out):
    phases, kinds = plan()
    nm = [0]
    nw = [0]
    na = [0]
    for k in kinds:
        na.append(na[-1] + (k == "P"))
        nm.append(nm[-1] + (k == "M"))
        nw.append(nw[-1] + (k == "W"))

    def phase(name, l):
        return next(x for x in phases if x.name == name and x.layer == l)

    with ExitStack() as ctx:
        at = [(nc.sbuf_base + 31) // 32 * 32]

        def place(name, shape, dt=F32, offset=None):
            size = int(np.prod(shape[1:])) * 4
            if offset is None:
                offset = at[0]
                at[0] += (size + 31) // 32 * 32
            return nc.alloc_sbuf_tensor_at(name, shape, dt, offset=offset)

        def end_of(offset, shape):
            return offset + (int(np.prod(shape[1:])) * 4 + 31) // 32 * 32

        x_sb = place("x_sb", [P, KT, T])
        hb = place("hb", [P, KT, 2 * T], F32R)
        whi = place("whi", [P, HSLOTS, 4, 512], F32R)
        ring = at[0]
        raw = place("raw", [P, SLOTS, 4, 512])
        wlo = place("wlo", [P, SLOTS, 4, 512], F32R, offset=ring)
        par_sb = place("par_sb", [P, V_N])
        mod = place("mod", [P, DEPTH * 6 * KT])
        ones = place("ones", [P, P])
        zeros = place("zeros", [P, 4])
        acc = place("acc", [P, 512])
        cact = place("cact", [P, KT])
        acol = place("acol", [P, KT])
        ada_raw = place("ada_raw", [P, ASLOTS, 512])
        scratch = at[0]
        ub = place("ub", [P, 4, T + 2])
        ssum = place("ssum", [P, T], offset=scratch)
        scratch = at[0]
        yb = place("yb", [P, 4, T])
        evb = place("evb", [P, BANKS, T], offset=scratch)
        acc2 = place("acc2", [P, 512], offset=scratch)
        arena = at[0]
        actb = place("actb", [P, FT, 2 * T], F32R)
        arena_end = at[0]
        assert arena_end <= nc.sbuf_usable_end, (arena_end, nc.sbuf_usable_end)
        cur = [arena]

        def inside(name, shape, dt=F32):
            t = place(name, shape, dt, offset=cur[0])
            cur[0] = end_of(cur[0], shape)
            assert cur[0] <= arena_end, name
            return t

        z = inside("z", [P, ZT, T])
        nrm = place("nrm", [P, KT, T], offset=arena)
        c_at = cur[0]
        c_sb = inside("c_sb", [P, C_N])
        pt = place("pt", [P, 2, 3 * P], offset=c_at + C_TRI * 4)
        ptc = place("ptc", [P, TB * P], offset=c_at + (C_TRI + 6 * P) * 4)
        assert 6 * P + TB * P <= C_CNEG - C_TRI
        wx_at = cur[0]
        wx = inside("wx", [P, KT, 32])
        wxlo = place("wxlo", [P, KT, 32], F32R, offset=wx_at)
        wxhi = inside("wxhi", [P, KT, 32], F32R)
        w2 = inside("w2", [P, 2, P])
        pos_sb = inside("pos_sb", [P, 2, CB])
        var = inside("var", [P, T])
        rstd = inside("rstd", [P, T])
        pr = place("pr", [P, 2, 2, 3 * P], offset=wx_at)
        assert end_of(wx_at, [P, 2, 2, 3 * P]) <= cur[0]
        lg = inside("lg", [P, TB, 32])
        eg = inside("eg", [P, TB, 32])
        gate = inside("gate", [P, TB, 3 * NSA])
        lf = inside("lf", [P, TB, FOX])
        ln1 = inside("ln1", [P, TB, FOX])
        gel = inside("gel", [P, KV * NC])
        kcT = inside("kcT", [P, KV * NC])
        vc = inside("vc", [P, KV, P])
        vsw_at = cur[0]
        vsw = inside("vsw", [P, 2, KV, TB, P])
        vf0 = place("vf0", [P, 4, P], offset=vsw_at)
        vf1 = place("vf1", [P, 2, P], offset=vsw_at + 4 * P * 4)
        Lb = inside("Lb", [P, T])
        Rall = inside("Rall", [P, T])
        rb_at = cur[0]
        Rb = inside("Rb", [P, 2, T])
        esum = place("esum", [P, T], offset=rb_at)
        ob = inside("ob", [P, NSA, 2 * T], F32R)
        xb = place("xb", [P, 2, CB, KV * NC], offset=arena + ZK * T * 4)
        rtmp = place("rtmp", [P, GROUP, T], offset=arena + ZV * T * 4)
        qn = inside("qn", [P, KV, T])
        prc = inside("prc", [P, TB, P])
        sc = inside("sc", [P, TB, 16])
        mx = inside("mx", [P, 3, TB])
        nb = inside("nb", [P, 3, TB])
        rs = inside("rs", [P, 3, TB])
        rr = inside("rr", [P, 3, TB])

        ps = ctx.enter_context(nc.psum_tensor("ps", [P, 8, 512], F32))

        sem = {}

        def S(name):
            if name not in sem:
                sem[name] = ctx.enter_context(nc.semaphore(name))
            return sem[name]

        full = [S(f"slot_full{n}") for n in range(SLOTS)]
        ada_full = [S(f"ada_full{n}") for n in range(ASLOTS)]
        acol_ready, sq_added = S("acol_ready"), S("sq_added")
        x_loaded, par_loaded, ext_loaded = S("x_loaded"), S("par_loaded"), S("ext_loaded")
        stored = S("stored")
        w_used, w1_used, ada_used, pre_used = S("w_used"), S("w1_used"), S("ada_used"), S("pre_used")
        hi_ready, lo_ready = S("hi_ready"), S("lo_ready")
        ada_sum, mod_ready = S("ada_sum"), S("mod_ready")
        bank_full, bank_free = S("bank_full"), S("bank_free")
        conv_y, conv_done, silu_done, prod_done, acthi, act_ready = (
            S(n) for n in ("conv_y", "conv_done", "silu_done", "prod_done", "acthi", "act_ready"))
        ehalf_ready, esum_ready, ext_t = S("ehalf_ready"), S("esum_ready"), S("ext_t")
        sq_ready, ss_ready, ssb_ready, var_ready, root_ready, t_ready, hh_ready, h_ready = (
            S(n) for n in ("sq_ready", "ss_ready", "ssb_ready", "var_ready", "root_ready", "t_ready",
                           "hh_ready", "h_ready"))
        hhi_ready = S("hhi_ready")
        x_done, cact_ready, ones_ready = S("x_done"), S("cact_ready"), S("ones_ready")
        dve_own, act_own, pool_own = S("dve_own"), S("act_own"), S("pool_own")
        xsq_ready, xhi_ready, xlo_ready, ext_sum, lg_ready, eg_ready, lf_ready, cum_ready, bias_ready = (
            S(n) for n in ("xsq_ready", "xhi_ready", "xlo_ready", "ext_sum", "lg_ready", "eg_ready", "lf_ready",
                           "cum_ready", "bias_ready"))
        xb_ready, gel_ready, cmp_ready, cmpc_ready, vsw_t, vsw_ready = (
            S(n) for n in ("xb_ready", "gel_ready", "cmp_ready", "cmpc_ready",
                           "vsw_t", "vsw_ready"))
        zero_ready, rope_ready, stage_ready, r_ready, s_ready, nb_ready, p_ready, pn_ready = (
            S(n) for n in ("zero_ready", "rope_ready", "stage_ready", "r_ready", "s_ready",
                           "nb_ready", "p_ready", "pn_ready"))
        pt_ready, ptc_ready, pv_ready, ohi_ready, o_done = (
            S(n) for n in ("pt_ready", "ptc_ready", "pv_ready", "ohi_ready", "o_done"))

        def modc(l, tile):
            return mod[:, l * 6 * KT + tile:l * 6 * KT + tile + 1]

        def flat(tile):
            return tile.rearrange("p o t -> p (o t)")

        def rows(w, k0, kn):
            return w[k0 * P:(k0 + kn) * P, :].rearrange("(k p) n -> p k n", p=P)

        def tiles_out(x, i=None):
            n = x.iters if i is None else i
            return n * (4 * x.groups) + (BANKS + 4 * x.g0)

        def n_of(l, n):
            return (NSA + FOX) * l + n

        block = ctx.enter_context(nc.Block())

        @block.sync
        def _(sp):
            def slot_wait(s, i, x):
                if s < SLOTS:
                    return
                who, counts = {"M": (w_used, nm), "W": (w1_used, nw), "P": (pre_used, na)}[kinds[s - SLOTS]]
                c1 = counts[s - SLOTS + 1]
                if isinstance(i, int):
                    sp.wait_ge(who, c1)
                else:
                    c2 = counts[s - SLOTS + x.r_per + 1]
                    sp.wait_ge(who, (i - 1) * (c2 - c1) + c1)

            def source(x, i, item):
                kind, g, q = item
                l = x.layer
                if kind == "W":
                    w = (w_cmp1_k, w_cmp1_v)[q // 2][l]
                    return w[(q % 2) * 16 * P:(q % 2 + 1) * 16 * P, :].rearrange("(j p) n -> p j n", p=P)
                if kind == "P":
                    return rows(w_ada, 4 * q, 4)[:, :, bass.ds(i * 1024 + g * 512, 512)]
                k0, kn = sum(x.ktiles[:q]), x.ktiles[q]
                if x.name in ("foxa", "foxb"):
                    return rows(w_in[l], k0, kn)[:, :, bass.ds(i * (512 * x.groups) + (x.first_group + g) * 512, 512)]
                if x.name in ("nsaa", "nsab"):
                    return rows(w_in[l], k0, kn)[:, :, bass.ds(i * 512 + ((x.first_group + g) * 512 + FF0 + FOX), 512)]
                if x.name in ("outn", "outf"):
                    return rows(w_out[l], k0 + (FOX if x.name == "outn" else 0), kn)[
                        :, :, bass.ds(i * (512 * x.groups) + g * 512, 512)]
                if x.name == "down":
                    return rows(w_down[l], k0, kn)[:, :, bass.ds(i * 512, 512)]
                return [rows(w_up[l], k0, kn)[:, :, bass.ds(i * 512 + (g * 256 + v * FF), 256)] for v in range(2)]

            def stream(x, i):
                for posn, item in enumerate(y for y in x.items if y[0] != "A"):
                    s = x.s0 + (i if isinstance(i, int) else 1) * x.r_per + posn
                    slot_wait(s, i, x)
                    slot = s % SLOTS
                    src = source(x, i, item)
                    if isinstance(src, list):
                        parts = [(raw[:, slot, :, v * 256:(v + 1) * 256], src[v]) for v in range(2)]
                    else:
                        n_rows = src.shape[1]
                        dst = raw[:, slot].rearrange("p k (j n) -> p (k j) n", n=P) if item[0] == "W" else raw[:, slot]
                        cut = (n_rows + 1) // 2
                        parts = [(dst[:, 0:cut], src[:, 0:cut]), (dst[:, cut:n_rows], src[:, cut:n_rows])]
                    for d_, s_ in parts:
                        sp.dma_start(d_, s_).then_inc(full[slot], 16)

            sp.dma_start(par_sb[:], par).then_inc(par_loaded, 16)
            for x in phases:
                stream(x, 0)
                if x.name == "pre":
                    sp.dma_start(x_sb[:], xT).then_inc(x_loaded, 16)
                if x.name == "nsaa":
                    l = x.layer
                    if l:
                        sp.wait_ge(x_done, 2 * l)
                    sp.dma_start(c_sb[:], consts).then_inc(ext_loaded, 16)
                    sp.dma_start(w2[:, 0, :], w_cmp2_k[l]).then_inc(ext_loaded, 16)
                    sp.dma_start(w2[:, 1, :], w_cmp2_v[l]).then_inc(ext_loaded, 16)
                    sp.dma_start(pos_sb[:], pos[l]).then_inc(ext_loaded, 16)
                    sp.dma_start(wx[:, :, 0:FOX], rows(w_in[l], 0, KT)[:, :, FF0:FF0 + FOX]).then_inc(ext_loaded, 16)
                    sp.dma_start(wx[:, :, FOX:32], rows(w_in[l], 0, KT)[:, :, NG0:D_IN]).then_inc(ext_loaded, 16)
                repeat(sp, 1, x.iters, lambda i, x=x: stream(x, i))
            for q in range(4):
                sp.wait_ge(hh_ready, 4 * (2 * DEPTH) + q + 1)
                sp.dma_start(out[:, 4 * q:4 * q + 4, :], nrm[:, 4 * q:4 * q + 4, :]).then_inc(stored, 16)
            sp.wait_ge(stored, 64)

        EXT = 6 * 16

        def ring_pos(x, posn):
            return sum(y[0] != "A" for y in x.items[:posn])

        def arrived(eng, x, i, posn):
            per, n = x.r_per // SLOTS, ring_pos(x, posn)
            eng.wait_ge(full[n % SLOTS], i * (32 * per) + 32 * (x.s0 // SLOTS + n // SLOTS + 1))

        def k_end(x, q):
            return sum(x.ktiles[:q + 1])

        def early_steps(x):
            if x.name not in ("nsaa", "outn", "outf", "up"):
                return []
            return [n for n, y in enumerate(x.items) if y[0] == "M"][:HSLOTS]

        def following(x):
            name, l = {"foxb": ("outn", x.layer), "outn": ("outf", x.layer), "outf": ("up", x.layer),
                       "down": ("nsaa", x.layer + 1)}.get(x.name, (None, 0))
            return phase(name, l) if name and l < DEPTH else None

        def ada_place(x, c):
            return (6, acc2) if x.name == "pre" and c == 1 else (7, acc)

        def m_pos(x, posn):
            return sum(y[0] == "M" for y in x.items[:posn])

        def m_index(x, i, posn):
            return i * x.m_per + (x.m0 + sum(y[0] == "M" for y in x.items[:posn]))

        def a_index(x, i, posn):
            return i * x.a_per + (x.a0 + tiles_of_ada(x.items[:posn]))

        def full_bank(eng, x, i, g, b):
            if b < BANKS - 1:
                eng.wait_ge(bank_full, i * (3 * x.groups) + (3 * (x.g0 + g) + b + 1))
            else:
                eng.wait_ge(w_used, i * x.m_per + (x.m0 + (g + 1) * (x.m_per // x.groups)))

        @block.tensor
        def _(pe):
            pe.wait_ge(ones_ready, 1)
            pe.wait_ge(cact_ready, 1)

            def main_step(x, i, posn):
                _, g, q = x.items[posn]
                m = m_index(x, i, posn)
                slot, high = ring_pos(x, posn) % SLOTS, m_pos(x, posn) % HSLOTS
                pe.wait_ge(lo_ready, m + 1)
                if x.name == "outn":
                    pe.wait_ge(o_done, n_of(x.layer, NSA - 1 + q))
                elif x.name == "outf":
                    pe.wait_ge(o_done, n_of(x.layer, NSA + k_end(x, q)))
                if x.name in ("nsaa", "up"):
                    pe.wait_ge(h_ready, 4 * (2 * x.layer + (x.name == "up")) + q + 1)
                if x.name == "down":
                    pe.wait_ge(act_ready, 1 + FT // 2 * x.layer + (sum(x.ktiles[:q + 1]) + 1) // 2)
                first, last = q == 0, q == len(x.ktiles) - 1
                k0, kn = sum(x.ktiles[:q]), x.ktiles[q]
                rhs = {"down": actb, "outn": ob}.get(x.name, hb)
                for b in range(BANKS):
                    if first:
                        pe.wait_ge(bank_free, i * (4 * x.groups) + (4 * (x.g0 + g) + b + 1))
                    for k in range(kn):
                        w = slice(b * P, (b + 1) * P)
                        pe.matmul(ps[:, b, 0:T], whi[:, high, k, w], rhs[:, k0 + k, 0:T],
                                  start=first and k == 0, stop=False)
                        pe.matmul(ps[:, b, 0:T], whi[:, high, k, w], rhs[:, k0 + k, T:2 * T], start=False, stop=False)
                        mm = pe.matmul(ps[:, b, 0:T], wlo[:, slot, k, w], rhs[:, k0 + k, 0:T],
                                       start=False, stop=last and k == kn - 1)
                    if last and b < BANKS - 1:
                        mm.then_inc(bank_full, 1)
                mm.then_inc(w_used, 1)

            def ada_total(x, i, posn, start=True):
                pe.wait_ge(ada_used, a_index(x, i, posn))
                if x.name == "foxa" and m_pos(x, posn) > 3:
                    pe.wait_ge(vsw_ready, x.layer + 1)
                elif x.name == "foxb" and not (isinstance(i, int) and i == 0):
                    pe.wait_ge(o_done, i * 2 + n_of(x.layer, 0))
                bank, sums = ada_place(x, x.items[posn - 1][1])
                for b in range(4):
                    mm = pe.matmul(ps[:, bank, b:b + 1], sums[:, b * P:(b + 1) * P], ones[:, 0:1],
                                   start=start, stop=start)
                if not start:
                    mm = pe.matmul(ps[:, bank, 0:4], ones[:], zeros[:], start=False, stop=True)
                mm.then_inc(ada_sum, 1)

            def ada_half(x, i, posn):
                _, c, r = x.items[posn]
                bank, _ = ada_place(x, c)
                arrived(pe, x, i, posn)
                if r == 0:
                    if not (isinstance(i, int) and i == 0):
                        pe.wait_ge(mod_ready, i * x.chunks + (c - 1))
                    pe.matmul(ps[:, bank, 0:4], ones[:], zeros[:], start=True, stop=False)
                for b in range(4):
                    if b == 3:
                        pe.wait_ge(ada_used, a_index(x, i, posn + 1))
                    mm = pe.matmul(ps[:, bank, b:b + 1], raw[:, ring_pos(x, posn) % SLOTS, 3, b * P:(b + 1) * P],
                                   cact[:, 4 * r + 3:4 * r + 4], start=False, stop=False)
                mm.then_inc(pre_used, 1)

            def chunk_ends(x, posn):
                for n in range(posn + 1, len(x.items)):
                    if x.items[n][0] == "M":
                        return None
                    if x.items[n][0] == "A" and x.items[n][2] == KT - 1:
                        return n + 1
                return None

            def run(x, after_step=None):
                def body(i):
                    for posn, item in enumerate(x.items):
                        if item[0] == "M":
                            main_step(x, i, posn)
                            end = chunk_ends(x, posn)
                            if end:
                                ada_total(x, i, end)
                            if after_step:
                                after_step(i, m_pos(x, posn))
                        elif item[0] == "P":
                            ada_half(x, i, posn)
                            if item[2] == KT // 4 - 1:
                                ada_total(x, i, posn + 1, start=False)
                if x.name == "pre":
                    body(0)
                    repeat(pe, 1, PRE_CUTS[0], body)
                    norm(0)
                    repeat(pe, PRE_CUTS[0], x.iters, body)
                elif after_step:
                    body(0)
                    repeat(pe, 1, x.iters, body)
                else:
                    repeat(pe, 0, x.iters, body)

            def norm(n):
                if n:
                    pe.wait_ge(sq_added, BANKS + KT * n)
                else:
                    pe.wait_ge(ss_ready, 1)
                pe.matmul(ps[:, 5, 0:T], ones[:], ssum[:], start=True, stop=True).then_inc(ssb_ready, 1)

            ident = c_sb[:, C_ID:C_ID + P]
            neg = c_sb[:, C_NEG:C_NEG + P]

            def prelude(l, step):
                if step == 0:
                    pe.wait_ge(xlo_ready, l + 1)
                    for k in range(KT):
                        pe.matmul(ps[0:32, 5, :], wxhi[:, k, :], hb[:, k, :], start=k == 0, stop=False)
                        mm = pe.matmul(ps[0:32, 5, T:2 * T], wxlo[:, k, :], hb[:, k, 0:T], start=False, stop=k == KT - 1)
                    mm.then_inc(ext_sum, 1)
                elif step == 2:
                    pe.wait_ge(esum_ready, l + 1)
                    for tb in range(TB):
                        mm = pe.transpose(ps[:, 5, tb * 32:tb * 32 + 32], esum[0:32, tb * P:(tb + 1) * P],
                                          c_sb[0:32, C_ID:C_ID + 32])
                    mm.then_inc(ext_t, 1)
                if step in HIDDEN:
                    n = HIDDEN.index(step)
                    kind, half = n // 2, n % 2
                    if step == HIDDEN[2]:
                        compressed(l, 0)
                    x = phase("nsab", l)
                    posn = x.items.index(("W", 0, n))
                    pe.wait_ge(xb_ready, 2 * l + kind + 1)
                    arrived(pe, x, 0, posn)
                    for j in range(16):
                        w = raw[:, ring_pos(x, posn) % SLOTS].rearrange("p k (j n) -> p (k j) n", n=P)[:, j, :]
                        mm = pe.matmul(ps[:, 4, 0:KV * NC], w, xb[:, kind, half * 16 + j, :],
                                       start=half == 0 and j == 0, stop=half == 1 and j == 15)
                    mm.then_inc(w1_used, 1)
                if step == 6:
                    pe.wait_ge(lf_ready, l + 1)
                    for tb in range(TB):
                        mm = pe.matmul(ps[0:FOX, 5, P:P + T], lf[:, tb, :],
                                       c_sb[:, C_TRI + tb * T:C_TRI + (tb + 1) * T],
                                       start=tb == 0, stop=tb == TB - 1)
                    mm.then_inc(cum_ready, 1)
                if step == 9:
                    compressed(l, 1)
                if step == 10:
                    pe.wait_ge(bank_free, tiles_out(phase("nsab", l)))
                    pe.wait_ge(cmpc_ready, 2 * l + 2)
                    pe.wait_ge(mod_ready, phase("foxa", l).first_chunk)
                    for n, tile in enumerate((ZVS, ZVW)):
                        for g in range(KV):
                            for tb in range(TB):
                                dst = ps[:, 6 + n, (g * TB + tb) * P:(g * TB + tb + 1) * P]
                                mm = pe.transpose(dst, z[:, tile + g, tb * P:(tb + 1) * P], ident)
                    mm.then_inc(vsw_t, 1)

            def compressed(l, kind):
                pe.wait_ge(gel_ready, 2 * l + kind + 1)
                if kind == 0:
                    mm = pe.matmul(ps[:, 6, 0:KV * NC], w2[:, 0, :], gel[:], start=True, stop=True)
                else:
                    pe.wait_ge(cmpc_ready, 2 * l + 1)
                    for g in range(KV):
                        mm = pe.matmul(ps[0:NC, 6, g * P:(g + 1) * P], gel[:, g * NC:(g + 1) * NC],
                                       w2[:, 1, :], start=True, stop=True)
                mm.then_inc(cmp_ready, 1)

            def scores(bank, q, keys, left=None, right=None):
                for m, (tb, kb) in enumerate(((0, 0), (1, 0), (1, 1))):
                    dst = ps[:, bank, m * P:(m + 1) * P]
                    diag = tb == kb
                    mm = pe.matmul(dst, q[:, tb * P:(tb + 1) * P], keys[:, kb * P:(kb + 1) * P],
                                   start=True, stop=not (left is not None or diag))
                    if left is not None:
                        mm = pe.matmul(dst, left[0:40, tb * P:(tb + 1) * P], right[0:40, kb * P:(kb + 1) * P],
                                       start=False, stop=not diag)
                    if diag:
                        mm = pe.matmul(dst, ident, neg, start=False, stop=True)
                return mm

            def nsa_scores(l, i, j):
                n = i * 2 + j
                if j == 0 and isinstance(i, int):
                    pe.wait_ge(cmpc_ready, 2 * l + 2)
                    pe.wait_ge(vsw_ready, l + 1)
                    pe.wait_ge(bias_ready, l + 1)
                else:
                    pe.wait_ge(p_ready, n + n_of(l, 0))
                pe.wait_ge(stage_ready, n + (NSA * l + 1))
                for tb in range(TB):
                    pe.matmul(ps[:, 5, T + P + tb * 16:T + P + tb * 16 + NC], qn[:, j, tb * P:(tb + 1) * P],
                              kcT[:, j * NC:(j + 1) * NC], start=True, stop=True)
                scores(5, qn[:, j], z[:, ZKS + j, :])
                scores(6, qn[:, j], z[:, ZKW + j, :]).then_inc(s_ready, 1)

            def turn_cs(l, i, j):
                n = i * 2 + j
                pe.wait_ge(pn_ready, n + n_of(l, 1))
                if l or not (isinstance(n, int) and n == 0):
                    pe.wait_ge(ptc_ready, n * 2 + 24 * l)
                for tb in range(TB):
                    pe.transpose(ps[:, 4, tb * P:(tb + 1) * P], prc[:, tb, :], ident)
                for m in range(2):
                    mm = pe.transpose(ps[:, 4, (m + 2) * P:(m + 3) * P], pr[:, j, 0, m * P:(m + 1) * P], ident)
                mm.then_inc(pt_ready, 1)

            def turn_sw(l, i, j):
                pe.wait_ge(ptc_ready, (i * 2 + j) * 2 + (24 * l + 1))
                pe.transpose(ps[:, 4, 0:P], pr[:, j, 0, 2 * P:3 * P], ident)
                for m in range(3):
                    mm = pe.transpose(ps[:, 4, (m + 1) * P:(m + 2) * P], pr[:, j, 1, m * P:(m + 1) * P], ident)
                mm.then_inc(pt_ready, 1)

            def nsa_values(l, i, j):
                n = i * 2 + j
                pe.wait_ge(ptc_ready, n * 2 + (24 * l + 2))
                if l or not (isinstance(n, int) and n == 0):
                    pe.wait_ge(o_done, n + n_of(l, 0))
                x = phase("foxb", l)
                if j == 0:
                    pe.wait_ge(mod_ready, i * x.chunks + (x.first_chunk + x.chunks))
                pe.matmul(ps[:, 7, 0:T], vc[0:NC, j, :], ptc[0:NC, :], start=True, stop=False)
                for u in range(2):
                    v, t = vsw[:, u, j], pt[:, u]
                    pe.matmul(ps[:, 7, P:T], v[:, 1, :], t[:, T:3 * P], start=False, stop=False)
                    mm = pe.matmul(ps[:, 7, 0:T], v[:, 0, :], t[:, 0:T], start=False, stop=u == 1)
                mm.then_inc(pv_ready, 1)

            def nsa_heads(l, i, step):
                later = not (isinstance(i, int) and i == 0)
                if step == 0:
                    if later:
                        nsa_values(l, i - 1, 0)
                        turn_cs(l, i - 1, 1)
                    nsa_scores(l, i, 0)
                elif step == 1 and later:
                    turn_sw(l, i - 1, 1)
                elif step == 2:
                    turn_cs(l, i, 0)
                    nsa_scores(l, i, 1)
                    if later:
                        nsa_values(l, i - 1, 1)
                elif step == 3:
                    turn_sw(l, i, 0)

            def fox_scores(l, h):
                pe.wait_ge(r_ready, FOX * l + h + 1)
                pe.wait_ge(p_ready, n_of(l, NSA + max(h - 1, 0)))
                pe.transpose(ps[:, 5 + h % 2, 3 * P:4 * P], z[:, ZV + h, 0:P], ident)
                scores(5 + h % 2, z[:, ZQ + h, :], z[:, ZK + h, :], Lb, Rb[:, h % 2, :]).then_inc(s_ready, 1)

            def fox_turn(l, h):
                pe.wait_ge(pn_ready, n_of(l, NSA + h + 1))
                pe.wait_ge(ptc_ready, 24 * l + 2 * NSA + h)
                pe.transpose(ps[:, 4, 0:P], z[:, ZV + h, P:T], ident)
                for m in range(3):
                    mm = pe.transpose(ps[:, 4, (m + 1) * P:(m + 2) * P], pr[:, h % 2, 0, m * P:(m + 1) * P], ident)
                mm.then_inc(pt_ready, 1)

            def fox_values(l, h):
                pe.wait_ge(ptc_ready, 24 * l + 2 * NSA + h + 1)
                pe.wait_ge(o_done, n_of(l, NSA + h))
                t = pt[:, h % 2]
                pe.matmul(ps[:, 7, 0:P], vf0[:, h % 4, :], t[:, 0:P], start=True, stop=True)
                pe.matmul(ps[:, 7, P:T], vf0[:, h % 4, :], t[:, P:T], start=True, stop=False)
                pe.matmul(ps[:, 7, P:T], vf1[:, h % 2, :], t[:, T:3 * P], start=False, stop=True).then_inc(pv_ready, 1)

            def fox_heads(l, step):
                for lag, part in ((3, fox_values), (2, fox_turn), (0, fox_scores)):
                    if 0 <= step - lag < FOX:
                        part(l, step - lag)

            for l in range(DEPTH):
                if l == 0:
                    run(phase("pre", 0))
                else:
                    norm(2 * l)
                run(phase("nsaa", l))
                run(phase("nsab", l), lambda i, step: prelude(l, step))
                run(phase("foxa", l), lambda i, step: prelude(l, 8 + step))
                run(phase("foxb", l), lambda i, step: nsa_heads(l, i, step))
                last = GROUP - 1
                nsa_values(l, last, 0)
                turn_cs(l, last, 1)
                fox_heads(l, 0)
                turn_sw(l, last, 1)
                fox_heads(l, 1)
                nsa_values(l, last, 1)
                run(phase("outn", l), lambda i, step: fox_heads(l, 4 * i + step + LEAD))
                run(phase("outf", l), lambda i, step: fox_heads(l, FOX + LEAD) if i == 0 and step == 0 else None)
                norm(2 * l + 1)
                run(phase("up", l))
                run(phase("down", l))
            norm(2 * DEPTH)

        @block.scalar
        def _(act):
            own = Chain(act, act_own)
            act.wait_ge(par_loaded, 16)
            act.activation(cact[:], par_sb[:, V_C:V_C + KT], ACT.Silu).then_inc(cact_ready, 1)

            def split_hi(x, i, posn):
                slot, m = ring_pos(x, posn) % SLOTS, m_pos(x, posn)
                kn = x.ktiles[x.items[posn][2]]
                arrived(act, x, i, posn)
                if not (isinstance(i, int) and i == 0 and x.m0 + m < HSLOTS):
                    act.wait_ge(w_used, i * x.m_per + (x.m0 + m - HSLOTS + 1))
                act.activation(whi[:, m % HSLOTS, 0:kn, :], raw[:, slot, 0:kn, :], ACT.Copy)\
                   .then_inc(hi_ready, 1)

            def early(x):
                for posn in early_steps(x):
                    split_hi(x, 0, posn)

            def out_plain(x, i, g, stage):
                if stage == 0 and x.name in ("nsaa", "nsab", "foxa", "foxb"):
                    first = 4 * (x.first_group + g) + (ZNQ if x.name in ("nsaa", "nsab") else 0)
                    for b in range(BANKS):
                        full_bank(act, x, i, g, b)
                        act.activation(flat(z[:, bass.ds(i * (4 * x.groups) + (first + b), 1), :]), ps[:, b, 0:T],
                                       ACT.Copy).then_inc(bank_free, 1)
                elif stage == 1 and x.name in ("outf", "down"):
                    for b in range(BANKS):
                        act.wait_ge(bank_free, i * (4 * x.groups) + (4 * (x.g0 + g) + b + 1 + BANKS))
                        act.wait_ge(sq_added, i * (BANKS * x.groups) + (x.r0 + BANKS * g + b + 1))
                        tile = i * (BANKS * x.groups) + (BANKS * g + b)
                        act.activation(evb[:, b, :], flat(x_sb[:, bass.ds(tile, 1), :]), ACT.Square)\
                           .then_inc(sq_ready, 1)

            def conv_col(l, tile, n):
                return par_sb[:, bass.ds(tile * 3 + (l * V_L + V_CW + n), 1)]

            def out_conv(x, i, g, stage):
                l = x.layer
                G = i * x.groups + g
                n0 = (x.layer) * (FT // 2)
                if stage == 0:
                    for b in range(BANKS):
                        full_bank(act, x, i, g, b)
                        act.wait_ge(conv_done, G * 1 + (n0 + 1))
                        act.activation(ub[:, b, 2:T + 2], ps[:, b, 0:T], ACT.Copy).then_inc(bank_free, 1)
                elif stage == 1:
                    for b in range(BANKS):
                        tile = G * 2 + (b % 2 + (b // 2) * FT)
                        if b == 0:
                            act.wait_ge(act_ready, G + (n0 + 1))
                        act.wait_ge(bank_free, i * (4 * x.groups) + (BANKS + 4 * (x.g0 + g) + b + 1))
                        act.activation(yb[:, b, :], ub[:, b, 2:T + 2], ACT.Identity,
                                       bias=par_sb[:, bass.ds(tile + (l * V_L + V_CB), 1)],
                                       scale=conv_col(l, tile, 2)).then_inc(conv_y, 1)
                elif stage == 2:
                    act.wait_ge(conv_done, G * 1 + (n0 + 2))
                    act.activation(yb[:, 0:2, :], yb[:, 0:2, :], ACT.Silu).then_inc(silu_done, 1)
                else:
                    act.wait_ge(prod_done, G * 1 + (n0 + 1))
                    act.activation(actb[:, bass.ds(G * 2, 2), 0:T], yb[:, 0:2, :], ACT.Copy).then_inc(acthi, 1)

            def evac(x, i, g, stage):
                (out_conv if x.name == "up" else out_plain)(x, i, g, stage)

            def run(x, beside=None):
                def body(i, first):
                    for posn, item in enumerate(x.items):
                        if item[0] == "M":
                            if not (first and posn in early_steps(x)):
                                split_hi(x, i, posn)
                            _, g, q = item
                            if beside and x.name == "outn":
                                beside(i, m_pos(x, posn))
                            if q < 4 and g:
                                evac(x, i, g - 1, q)
                            elif q < 4 and not first:
                                evac(x, i - 1, x.groups - 1, q)
                            elif q < 4 and x.after:
                                evac(x.after, x.after.iters - 1, x.after.groups - 1, q)
                            if beside and x.name != "outn":
                                beside(i, m_pos(x, posn))
                if x.m_per:
                    body(0, True)
                    repeat(act, 1, x.iters, lambda i: body(i, False))
                    if following(x):
                        split_hi(following(x), 0, 0)
                    if x.name in ("foxb", "outn"):
                        beside(x.iters, 0)
                    if not x.hands_on:
                        for stage in range(4):
                            evac(x, x.iters - 1, x.groups - 1, stage)

            def norm(n):
                final = n == 2 * DEPTH
                l = n // 2
                if n == 0:
                    act.wait_ge(x_loaded, 16)
                    act.activation(nrm[:], x_sb[:], ACT.Square).then_inc(xsq_ready, 1)
                act.wait_ge(var_ready, n + 1)
                act.activation(rstd[:], var[:], ACT.Sqrt).then_inc(root_ready, 1)
                shift = M_SHF if n % 2 else M_SHA
                if not final:
                    act.wait_ge(acol_ready, n + 1)
                for q in range(4):
                    act.wait_ge(t_ready, 4 * n + q + 1)
                    for k in range(4 * q, 4 * q + 4):
                        if final:
                            a = act.activation(nrm[:, k, :], nrm[:, k, :], ACT.Copy, scale=par_sb[:, V_FIN + k:V_FIN + k + 1])
                        else:
                            a = act.activation(nrm[:, k, :], nrm[:, k, :], ACT.Identity, bias=modc(l, shift + k),
                                               scale=acol[:, k:k + 1])
                    a.then_inc(hh_ready, 1)
                    if not final:
                        act.wait_ge(hh_ready, 4 * n + q + 1)
                        act.activation(hb[:, 4 * q:4 * q + 4, 0:T], nrm[:, 4 * q:4 * q + 4, :], ACT.Copy)\
                           .then_inc(hhi_ready, 1)
                    if n == 0 and q == 0:
                        early(phase("nsaa", 0))

            def prelude(l, step):
                if step == 0:
                    act.wait_ge(ext_loaded, EXT * (l + 1))
                    act.activation(wxhi[:], wx[:], ACT.Copy).then_inc(xhi_ready, 1)
                elif step == 2:
                    act.wait_ge(ext_sum, l + 1)
                    act.activation(esum[0:32, :], ps[0:32, 5, T:2 * T], ACT.Copy).then_inc(ehalf_ready, 1)
                elif step == 4:
                    act.wait_ge(lg_ready, l + 1)
                    own(act.activation(ln1[:], lg[:, :, 0:FOX], ACT.Abs))
                    own(act.activation(ln1[:], ln1[:], ACT.Exp, scale=-1.0))
                    act.activation(eg[:, :, FOX:32], lg[:, :, FOX:32], ACT.Exp, scale=-1.0)
                    act.activation(ln1[:], ln1[:], ACT.Ln, bias=1.0).then_inc(eg_ready, 1)
                elif step in (6, 9):
                    kind = int(step == 9)
                    act.wait_ge(w1_used, 4 * l + 2 * kind + 2)
                    if kind:
                        act.wait_ge(cmp_ready, 2 * l + 1)
                    act.activation(gel[:], ps[:, 4, 0:KV * NC], ACT.Gelu_apprx_tanh).then_inc(gel_ready, 1)
                elif step == 12:
                    act.wait_ge(vsw_t, l + 1)
                    for n in range(2):
                        a = act.activation(vsw[:, n].rearrange("p g t d -> p (g t d)"), ps[:, 6 + n, :], ACT.Copy)
                    a.then_inc(vsw_ready, 1)

            def stage(l, i, j):
                act.activation(qn[:, j, :], flat(z[:, bass.ds(i + (ZNQ + GROUP * j), 1), :]), ACT.Copy)\
                   .then_inc(stage_ready, 1)

            def nsa_exp(l, i, j):
                act.wait_ge(nb_ready, i * 2 + n_of(l, j + 1))
                act.activation(sc[:, :, 0:NC], sc[:, :, 0:NC], ACT.Exp, scale=SCALE)
                for u in (1, 2):
                    act.activation(pr[:, j, u - 1, 0:P], ps[:, 4 + u, 0:P], ACT.Exp, bias=nb[:, u, 0:1],
                                   scale=SCALE, accum_out=rs[:, u, 0:1])
                    a = act.activation(pr[:, j, u - 1, P:3 * P], ps[:, 4 + u, P:3 * P], ACT.Exp, bias=nb[:, u, 1:2],
                                       scale=SCALE, accum_out=rs[:, u, 1:2])
                a.then_inc(p_ready, 1)

            def copy_cs(l, i, j):
                act.wait_ge(pt_ready, i * 4 + (24 * l + 2 * j + 1))
                act.activation(ptc[:], ps[:, 4, 0:TB * P], ACT.Copy)
                act.activation(pt[:, 0, 0:T], ps[:, 4, T:2 * T], ACT.Copy).then_inc(ptc_ready, 1)

            def copy_sw(l, i, j):
                act.wait_ge(pt_ready, i * 4 + (24 * l + 2 * j + 2))
                act.activation(pt[:].rearrange("p u n -> p (u n)")[:, T:6 * P], ps[:, 4, :], ACT.Copy)\
                   .then_inc(ptc_ready, 1)

            def nsa_high(l, i, j):
                act.wait_ge(pv_ready, i * 2 + n_of(l, j + 1))
                act.activation(flat(ob[:, bass.ds(i + GROUP * j, 1), 0:T]), ps[:, 7, 0:T], ACT.Copy)\
                   .then_inc(ohi_ready, 1)

            def nsa_heads(l, i, step):
                later = not (isinstance(i, int) and i == 0)
                there = not (isinstance(i, int) and i == GROUP)
                if step == 0:
                    if later:
                        copy_cs(l, i - 1, 0)
                        nsa_exp(l, i - 1, 1)
                    if there:
                        if not later:
                            act.wait_ge(rope_ready, l + 1)
                        stage(l, i, 0)
                elif step == 1 and later:
                    copy_sw(l, i - 1, 0)
                    nsa_high(l, i - 1, 0)
                elif step == 2:
                    if later:
                        copy_cs(l, i - 1, 1)
                    if there:
                        nsa_exp(l, i, 0)
                        stage(l, i, 1)
                elif step == 3 and later:
                    copy_sw(l, i - 1, 1)
                    nsa_high(l, i - 1, 1)

            def fox_exp(l, h):
                act.wait_ge(nb_ready, n_of(l, NSA + h + 1))
                p, bank = h % 2, 5 + h % 2
                act.activation(vf0[:, h % 4, :], ps[:, bank, 3 * P:4 * P], ACT.Copy)
                act.activation(pr[:, p, 0, 0:P], ps[:, bank, 0:P], ACT.Exp, bias=nb[:, 1, 0:1],
                               scale=SCALE, accum_out=rs[:, 1, 0:1])
                act.activation(pr[:, p, 0, P:3 * P], ps[:, bank, P:3 * P], ACT.Exp, bias=nb[:, 1, 1:2],
                               scale=SCALE, accum_out=rs[:, 1, 1:2]).then_inc(p_ready, 1)

            def fox_copy(l, h):
                act.wait_ge(pt_ready, 24 * l + 2 * NSA + h + 1)
                act.activation(vf1[:, h % 2, :], ps[:, 4, 0:P], ACT.Copy)
                act.activation(pt[:, h % 2, :], ps[:, 4, P:4 * P], ACT.Copy).then_inc(ptc_ready, 1)

            def fox_high(l, h):
                act.wait_ge(pv_ready, n_of(l, NSA + h + 1))
                act.activation(hb[:, h, 0:T], ps[:, 7, 0:T], ACT.Copy).then_inc(ohi_ready, 1)

            def fox_heads(l, step):
                for lag, part in ((4, fox_copy), (2, fox_exp), (5, fox_high)):
                    if 0 <= step - lag < FOX:
                        part(l, step - lag)

            for l in range(DEPTH):
                norm(2 * l)
                run(phase("nsaa", l))
                run(phase("nsab", l), lambda i, step: prelude(l, step))
                run(phase("foxa", l), lambda i, step: prelude(l, 8 + step))
                run(phase("foxb", l), lambda i, step: nsa_heads(l, i, step))
                nsa_heads(l, GROUP, 1)
                nsa_heads(l, GROUP, 2)
                split_hi(phase("outn", l), 0, 1)
                nsa_heads(l, GROUP, 3)
                run(phase("outn", l), lambda i, step: fox_heads(l, 4 * i + step + LEAD))
                fox_heads(l, FOX + LEAD + 1)
                split_hi(phase("outf", l), 0, 1)
                fox_heads(l, FOX + LEAD + 2)
                run(phase("outf", l))
                split_hi(phase("up", l), 0, 1)
                norm(2 * l + 1)
                run(phase("up", l))
                run(phase("down", l))
                if l + 1 < DEPTH:
                    split_hi(phase("nsaa", l + 1), 0, 1)
            norm(2 * DEPTH)

        @block.vector
        def _(dve):
            own = Chain(dve, dve_own)
            dve.sem_inc(bank_free, BANKS)
            dve.sem_inc(conv_done, 1)
            dve.sem_inc(sq_added, BANKS)
            dve.sem_inc(act_ready, 1)
            dve.memset(zeros[:], 0.0)
            dve.memset(ones[:], 1.0).then_inc(ones_ready, 1)
            dve.wait_ge(cact_ready, 1)

            def split_lo(x, i, posn):
                kn = x.ktiles[x.items[posn][2]]
                slot, high = ring_pos(x, posn) % SLOTS, m_pos(x, posn) % HSLOTS
                dve.wait_ge(hi_ready, m_index(x, i, posn) + 1)
                dve.tensor_tensor(wlo[:, slot, 0:kn, :], raw[:, slot, 0:kn, :],
                                  whi[:, high, 0:kn, :].bitcast(F32), ALU.subtract).then_inc(lo_ready, 1)

            def early(x):
                for posn in early_steps(x):
                    split_lo(x, 0, posn)

            def ada_step(x, i, posn):
                kind, _, kt = x.items[posn]
                if kind == "A":
                    n = sum(y[0] == "A" for y in x.items[:posn])
                    slot, per = n % ASLOTS, x.b_per // ASLOTS
                    dve.wait_ge(ada_full[slot], i * (16 * per) + 16 * (x.b0 // ASLOTS + n // ASLOTS + 1))
                    tiles = [(kt, ada_raw[:, slot, :])]
                else:
                    arrived(dve, x, i, posn)
                    tiles = [(4 * kt + k, raw[:, ring_pos(x, posn) % SLOTS, k, :]) for k in range(3)]
                _, sums = ada_place(x, x.items[posn][1])
                for n, (k, tile) in enumerate(tiles):
                    c = cact[:, k:k + 1]
                    if k == 0:
                        a = dve.tensor_scalar(sums[:], tile, c, None, ALU.mult)
                    else:
                        dve.wait_ge(ada_used, a_index(x, i, posn) + n)
                        a = dve.scalar_tensor_tensor(out=sums[:], in0=tile, scalar=c, in1=sums[:],
                                                     op0=ALU.mult, op1=ALU.add)
                    a.then_inc(ada_used, 1)

            def ada_out(x, i, c):
                first = x.first_chunk + c
                dve.wait_ge(ada_sum, i * x.chunks + (first + 1))
                col = i * (4 * x.chunks) + first * 4
                bank, _ = ada_place(x, c)
                dve.tensor_tensor(mod[:, bass.ds(col, 4)], ps[:, bank, 0:4],
                                  par_sb[:, bass.ds(col + V_BA, 4)], ALU.add).then_inc(mod_ready, 1)
                dve.wait_ge(mod_ready, i * x.chunks + (first + 1))

            def out_plain(x, i, g, stage):
                l = x.layer
                if stage == 0 and x.name in ("outn", "outf", "down"):
                    for b in range(BANKS):
                        full_bank(dve, x, i, g, b)
                        tile = i * (4 * x.groups) + (4 * g + b)
                        gate_ = mod[:, bass.ds(tile + (6 * KT * l + (M_GF if x.name == "down" else M_GA)), 1)]
                        xt = flat(x_sb[:, bass.ds(tile, 1), :])
                        dve.scalar_tensor_tensor(out=xt, in0=ps[:, b, 0:T], scalar=gate_, in1=xt,
                                                 op0=ALU.mult, op1=ALU.add).then_inc(bank_free, 1)
                elif stage == 1 and x.name in ("outf", "down"):
                    for b in range(BANKS):
                        n = i * (BANKS * x.groups) + (x.r0 + BANKS * g + b + 1)
                        dve.wait_ge(sq_ready, n)
                        dve.wait_ge(sq_added, n + (BANKS - 1))
                        dve.tensor_tensor(ssum[:], ssum[:], evb[:, b, :], ALU.add).then_inc(sq_added, 1)

            def conv_col(l, tile, n):
                return par_sb[:, bass.ds(tile * 3 + (l * V_L + V_CW + n), 1)]

            def out_conv(x, i, g, stage):
                l = x.layer
                G = i * x.groups + g
                n0 = l * (FT // 2)
                if stage == 1:
                    for tap in (1, 0):
                        for b in range(BANKS):
                            tile = G * 2 + (b % 2 + (b // 2) * FT)
                            if tap == 1:
                                dve.wait_ge(conv_y, G * 4 + (4 * n0 + b + 1))
                            a = dve.scalar_tensor_tensor(out=yb[:, b, :], in0=ub[:, b, tap:T + tap],
                                                         scalar=conv_col(l, tile, tap), in1=yb[:, b, :],
                                                         op0=ALU.mult, op1=ALU.add)
                            if tap == 1:
                                if b == BANKS - 1:
                                    own(a)
                            elif b == BANKS - 1:
                                a.then_inc(conv_done, 1)
                elif stage == 2:
                    dve.wait_ge(silu_done, G * 1 + (n0 + 1))
                    dve.tensor_tensor(yb[:, 0:2, :], yb[:, 0:2, :], yb[:, 2:4, :], ALU.mult).then_inc(prod_done, 1)
                elif stage == 3:
                    dve.wait_ge(acthi, G * 1 + (n0 + 1))
                    hi = actb[:, bass.ds(G * 2, 2), 0:T]
                    dve.tensor_tensor(actb[:, bass.ds(G * 2, 2), T:2 * T], yb[:, 0:2, :], hi.bitcast(F32), ALU.subtract)\
                       .then_inc(act_ready, 1)

            def evac(x, i, g, stage):
                (out_conv if x.name == "up" else out_plain)(x, i, g, stage)

            def run(x, beside=None, waits=0):
                ends_late = x.m_per and x.chunks and x.items[-1][0] == "A"

                def body(i, first):
                    pending = None if first or not ends_late else (x, i - 1, x.chunks - 1)
                    if first and late:
                        pending = late.pop()
                    step = None
                    for posn, item in enumerate(x.items):
                        if item[0] == "M":
                            if beside and step is not None:
                                beside(i, step, True)
                            step = m_pos(x, posn)
                            if not (first and posn in early_steps(x)):
                                split_lo(x, i, posn)
                            _, g, q = item
                            if beside and x.name == "outn":
                                beside(i, step, False)
                            if q < 4 and g:
                                evac(x, i, g - 1, q)
                            elif q < 4 and not first:
                                evac(x, i - 1, x.groups - 1, q)
                            elif q < 4 and x.after:
                                evac(x.after, x.after.iters - 1, x.after.groups - 1, q)
                            if first and g == 0 and q == len(x.ktiles) - 1 and x.name in ("outf", "down"):
                                own(dve.memset(ssum[:], 0.0))
                            if pending:
                                ada_out(*pending)
                                pending = None
                            if beside and x.name != "outn":
                                beside(i, step, False)
                        elif item[0] == "A":
                            ada_step(x, i, posn)
                            if item[2] == KT - 1:
                                pending = (x, i, item[1])
                        elif item[0] == "P":
                            ada_step(x, i, posn)
                            if item[1:] == (1, 0):
                                ada_out(x, i, 0)
                            elif item[1:] == (0, 0) and not first:
                                ada_out(x, i - 1, 1)
                    if beside and x.m_per:
                        beside(i, step, True)
                    assert pending is None or ends_late or not x.m_per

                if not x.m_per:
                    for n, (start, end) in enumerate(zip((0,) + PRE_CUTS, PRE_CUTS + (x.iters,))):
                        repeat(dve, start, end, lambda i: body(i, start == 0))
                        if end == x.iters:
                            ada_out(x, x.iters - 1, 1)
                        beside(n)
                    return
                body(0, True)
                per = waits + x.groups * (x.name == "up")
                own.loop(1, x.iters, per, lambda i: body(i, False))
                if ends_late:
                    late.append((x, x.iters - 1, x.chunks - 1))
                if following(x):
                    split_lo(following(x), 0, 0)
                if x.name in ("foxb", "outn"):
                    beside(x.iters, 0, False)
                if not x.hands_on:
                    for stage in range(4):
                        evac(x, x.iters - 1, x.groups - 1, stage)
                    flush()

            late = []

            def flush():
                if late:
                    ada_out(*late.pop())

            def norm(n):
                final = n == 2 * DEPTH
                if n == 0:
                    def part(step):
                        if step == 0:
                            dve.wait_ge(xsq_ready, 1)
                            dve.tensor_reduce(ssum[:], nrm[:].rearrange("p k t -> p t k"), AX.X, ALU.add)\
                               .then_inc(ss_ready, 1)
                        elif step == 1:
                            root(0)
                            normed(0, 0)
                        elif step == 2:
                            normed(0, 1)
                            normed(0, 2)
                        else:
                            column_scale(0)
                    run(phase("pre", 0), part)
                    low(0, 0)
                    early(phase("nsaa", 0))
                    normed(0, 3)
                    low(0, 1)
                    low(0, 2)
                else:
                    column_scale(n)
                    root(n)
                    for q in range(4):
                        normed(n, q)
                        if not final and q == 1:
                            split_lo(phase("up", n // 2) if n % 2 else phase("nsaa", n // 2), 0, 1)
                        if not final and q:
                            low(n, q - 1)
                if not final:
                    low(n, 3)

            def root(n):
                dve.wait_ge(ssb_ready, n + 1)
                dve.tensor_scalar(var[:], ps[:, 5, 0:T], 1.0 / D, EPS, ALU.mult, ALU.add).then_inc(var_ready, 1)
                dve.wait_ge(root_ready, n + 1)
                own(dve.reciprocal(rstd[:], rstd[:]))

            def normed(n, q):
                dve.tensor_tensor(nrm[:, 4 * q:4 * q + 4, :], x_sb[:, 4 * q:4 * q + 4, :],
                                  rstd[:].unsqueeze(1).broadcast_to([P, 4, T]), ALU.mult).then_inc(t_ready, 1)

            def column_scale(n):
                if n == 2 * DEPTH:
                    return
                l = n // 2
                gain = V_GF if n % 2 else V_GA
                scl = M_SCF if n % 2 else M_SCA
                dve.scalar_tensor_tensor(out=acol[:], in0=mod[:, l * 6 * KT + scl:l * 6 * KT + scl + KT], scalar=1.0,
                                         in1=par_sb[:, l * V_L + gain:l * V_L + gain + KT],
                                         op0=ALU.add, op1=ALU.mult).then_inc(acol_ready, 1)

            def low(n, q):
                dve.wait_ge(hhi_ready, 4 * n + q + 1)
                hi = hb[:, 4 * q:4 * q + 4, 0:T].bitcast(F32)
                dve.tensor_tensor(hb[:, 4 * q:4 * q + 4, T:2 * T], nrm[:, 4 * q:4 * q + 4, :], hi, ALU.subtract)\
                   .then_inc(h_ready, 1)

            def rope(t0, n):
                zz = z[:, t0:t0 + n, :]
                half = HD // 2
                for a, b in ((0, half), (half, 0)):
                    sin = c_sb[b:b + half, C_SIN:C_SIN + T].unsqueeze(1).broadcast_to([half, n, T])
                    last = dve.tensor_tensor(rtmp[a:a + half, 0:n, :], z[b:b + half, t0:t0 + n, :], sin, ALU.mult)
                    own(last)
                cos = c_sb[:, C_COS:C_COS + T].unsqueeze(1).broadcast_to([P, n, T])
                own(dve.tensor_tensor(zz, zz, cos, ALU.mult))
                own(dve.tensor_tensor(zz, zz, rtmp[:, 0:n, :], ALU.add))

            def blocks(kind, l):
                for g in range(KV):
                    tile = z[:, (ZVC if kind else ZKC) + g, :]
                    for half in range(2):
                        src = tile[:, half * 16:half * 16 + NC * CS].rearrange("p (n j) -> p j n", j=CS)
                        ps_ = pos_sb[:, kind, half * 16:half * 16 + 16].unsqueeze(2).broadcast_to([P, 16, NC])
                        a = dve.tensor_tensor(xb[:, kind, half * 16:half * 16 + 16, g * NC:(g + 1) * NC], src, ps_, ALU.add)
                a.then_inc(xb_ready, 1)

            cneg = c_sb[:, C_CNEG:C_CNEG + 32].rearrange("p (t n) -> p t n", t=TB)[:, :, 0:NC]
            c01 = c_sb[:, C_C01:C_C01 + 32].rearrange("p (t n) -> p t n", t=TB)[:, :, 0:NC]

            def prelude(l, step, after):
                if after:
                    return
                if step == 0:
                    dve.wait_ge(xhi_ready, l + 1)
                    dve.tensor_tensor(wxlo[:], wx[:], wxhi[:].bitcast(F32), ALU.subtract).then_inc(xlo_ready, 1)
                    dve.wait_ge(bank_free, tiles_out(phase("nsaa", l)))
                    rope(ZKC, KV)
                elif step == 1:
                    blocks(0, l)
                    blocks(1, l)
                elif step == 2:
                    dve.wait_ge(ehalf_ready, l + 1)
                    dve.tensor_tensor(esum[0:32, :], ps[0:32, 5, 0:T], esum[0:32, :], ALU.add).then_inc(esum_ready, 1)
                elif step == 4:
                    dve.wait_ge(ext_t, l + 1)
                    e = ps[:, 5, 0:64].rearrange("p (t n) -> p t n", t=TB)
                    bf = par_sb[:, l * V_L + V_BF:l * V_L + V_BF + FOX].unsqueeze(1).broadcast_to([P, TB, FOX])
                    dve.tensor_tensor(lg[:, :, 0:FOX], e[:, :, 0:FOX], bf, ALU.add)
                    dve.tensor_scalar(lg[:, :, FOX:32], e[:, :, FOX:32], 1.0, None, ALU.mult).then_inc(lg_ready, 1)
                elif step == 5:
                    dve.wait_ge(eg_ready, l + 1)
                    own(dve.tensor_scalar(gate[:], eg[:, :, FOX:32], 1.0, None, ALU.add))
                    own(dve.reciprocal(gate[:], gate[:]))
                    own(dve.tensor_scalar(lf[:], lg[:, :, 0:FOX], 0.0, ROOT, ALU.min, ALU.mult))
                    dve.scalar_tensor_tensor(out=lf[:], in0=ln1[:], scalar=-ROOT, in1=lf[:], op0=ALU.mult, op1=ALU.add)\
                       .then_inc(lf_ready, 1)
                elif step in (3, 6, 7):
                    rope(ZNQ + 2 * (3, 6, 7).index(step), 2)
                elif step == 8:
                    rope(ZNQ + 6, 2)
                    dve.wait_ge(cum_ready, l + 1)
                    dve.wait_ge(zero_ready, l + 1)
                    cum = ps[0:FOX, 5, P:P + T]
                    own(dve.tensor_scalar(Rall[0:FOX, :], cum, -1.0, None, ALU.mult))
                    dve.tensor_scalar(Lb[32:32 + FOX, :], cum, 1.0, None, ALU.mult).then_inc(bias_ready, 1)
                elif step == 9:
                    dve.wait_ge(cmp_ready, 2 * l + 1)
                    dve.tensor_copy(kcT[:], ps[:, 6, 0:KV * NC]).then_inc(cmpc_ready, 1)
                elif step == 10:
                    dve.wait_ge(bank_free, tiles_out(phase("nsab", l)))
                    rope(ZKS, KV)
                elif step == 11:
                    dve.wait_ge(cmp_ready, 2 * l + 2)
                    dve.tensor_copy(vc[0:NC].rearrange("p g d -> p (g d)"), ps[0:NC, 6, 0:KV * P])\
                       .then_inc(cmpc_ready, 1)
                elif step == 12:
                    rope(ZKW, KV)
                    dve.sem_inc(rope_ready, 1)
                elif step == 13:
                    own(dve.memset(prc[:], 0.0))

            def nsa_top(l, i, j):
                dve.wait_ge(s_ready, i * 2 + n_of(l, j + 1))
                s = ps[:, 5, T + P:T + P + 32].rearrange("p (t n) -> p t n", t=TB)[:, :, 0:NC]
                own(dve.tensor_tensor(sc[:, :, 0:NC], s, cneg, ALU.add))
                dve.tensor_reduce(mx[:, 0, :], sc[:, :, 0:NC], AX.X, ALU.max)
                for u in (1, 2):
                    dve.tensor_reduce(mx[:, u, 0:1], ps[:, 4 + u, 0:P], AX.X, ALU.max)
                    a = dve.tensor_reduce(mx[:, u, 1:2], ps[:, 4 + u, P:3 * P], AX.X, ALU.max)
                own(a)
                for tb in range(TB):
                    dve.tensor_scalar(sc[:, tb, 0:NC], sc[:, tb, 0:NC], mx[:, 0, tb:tb + 1], None, ALU.subtract)
                dve.tensor_scalar(nb[:, 1:3, :], mx[:, 1:3, :], -SCALE, None, ALU.mult).then_inc(nb_ready, 1)

            def nsa_scale(l, i, j):
                dve.wait_ge(p_ready, i * 2 + n_of(l, j + 1))
                own(dve.tensor_tensor(sc[:, :, 0:NC], sc[:, :, 0:NC], c01, ALU.mult))
                own(dve.tensor_reduce(rs[:, 0, :], sc[:, :, 0:NC], AX.X, ALU.add))
                own(dve.tensor_scalar(rr[:], rs[:], TINY, None, ALU.max))
                own(dve.reciprocal(rr[:], rr[:]))
                g = gate[:, :, bass.ds(i * 3 + 3 * GROUP * j, 3)].rearrange("p t n -> p n t")
                own(dve.tensor_tensor(rr[:], rr[:], g, ALU.mult))
                if l or j or not isinstance(i, int):
                    dve.wait_ge(pt_ready, i * 4 + (24 * l + 2 * j - 1))
                for tb in range(TB):
                    dve.tensor_scalar(prc[:, tb, 0:NC], sc[:, tb, 0:NC], rr[:, 0, tb:tb + 1], None, ALU.mult)
                    for u in (1, 2):
                        cols = pr[:, j, u - 1, 0:P] if tb == 0 else pr[:, j, u - 1, P:3 * P]
                        a = dve.tensor_scalar(cols, cols, rr[:, u, tb:tb + 1], None, ALU.mult)
                a.then_inc(pn_ready, 1)

            def nsa_low(l, i, j):
                dve.wait_ge(ohi_ready, i * 2 + n_of(l, j + 1))
                tile = bass.ds(i + GROUP * j, 1)
                dve.tensor_tensor(flat(ob[:, tile, T:2 * T]), ps[:, 7, 0:T], flat(ob[:, tile, 0:T]).bitcast(F32),
                                  ALU.subtract).then_inc(o_done, 1)

            def nsa_heads(l, i, step, after):
                later = not (isinstance(i, int) and i == 0)
                there = not (isinstance(i, int) and i == GROUP)
                part = nsa_scale if after else nsa_top
                if step == 0 and later:
                    part(l, i - 1, 1)
                elif step == 2 and there:
                    part(l, i, 0)
                elif step in (1, 3) and after and later:
                    nsa_low(l, i - 1, step // 2)

            def fox_right(l, h):
                if h > 1:
                    dve.wait_ge(s_ready, n_of(l, NSA + h - 1))
                dve.tensor_scalar(Rb[0:40, h % 2, :], Rall[0:40, :], c_sb[0:40, C_SEL + h:C_SEL + h + 1], None, ALU.mult)\
                   .then_inc(r_ready, 1)

            def fox_top(l, h):
                dve.wait_ge(s_ready, n_of(l, NSA + h + 1))
                bank = 5 + h % 2
                dve.tensor_reduce(mx[:, 1, 0:1], ps[:, bank, 0:P], AX.X, ALU.max)
                own(dve.tensor_reduce(mx[:, 1, 1:2], ps[:, bank, P:3 * P], AX.X, ALU.max))
                dve.tensor_scalar(nb[:, 1, :], mx[:, 1, :], -SCALE, None, ALU.mult).then_inc(nb_ready, 1)

            def fox_scale(l, h):
                dve.wait_ge(p_ready, n_of(l, NSA + h + 1))
                own(dve.tensor_scalar(rr[:, 1, :], rs[:, 1, :], TINY, None, ALU.max))
                own(dve.reciprocal(rr[:, 1, :], rr[:, 1, :]))
                for tb in range(TB):
                    cols = pr[:, h % 2, 0, 0:P] if tb == 0 else pr[:, h % 2, 0, P:3 * P]
                    a = dve.tensor_scalar(cols, cols, rr[:, 1, tb:tb + 1], None, ALU.mult)
                a.then_inc(pn_ready, 1)

            def fox_low(l, h):
                dve.wait_ge(ohi_ready, n_of(l, NSA + h + 1))
                dve.tensor_tensor(hb[:, h, T:2 * T], ps[:, 7, 0:T], hb[:, h, 0:T].bitcast(F32), ALU.subtract)\
                   .then_inc(o_done, 1)

            def fox_heads(l, step, after):
                for lag, part in ((2, fox_scale), (5, fox_low)) if after else ((0, fox_right), (2, fox_top)):
                    if 0 <= step - lag < FOX:
                        part(l, step - lag)

            for l in range(DEPTH):
                norm(2 * l)
                run(phase("nsaa", l))
                run(phase("nsab", l), lambda i, step, after: prelude(l, step, after))
                run(phase("foxa", l), lambda i, step, after: prelude(l, 8 + step, after))
                run(phase("foxb", l), lambda i, step, after: nsa_heads(l, i, step, after), 14)
                nsa_heads(l, GROUP, 0, True)
                for step in range(LEAD):
                    fox_heads(l, step, False)
                nsa_heads(l, GROUP, 1, True)
                split_lo(phase("outn", l), 0, 1)
                nsa_heads(l, GROUP, 3, True)
                run(phase("outn", l), lambda i, step, after: fox_heads(l, 4 * i + step + LEAD, after), 12)
                fox_heads(l, FOX + LEAD, True)
                fox_heads(l, FOX + LEAD + 1, True)
                split_lo(phase("outf", l), 0, 1)
                fox_heads(l, FOX + LEAD + 2, True)
                run(phase("outf", l))
                dve.wait_ge(bank_free, tiles_out(phase("outf", l)))
                dve.sem_inc(x_done, 1)
                norm(2 * l + 1)
                own(dve.memset(ub[:, :, 0:2], 0.0))
                run(phase("up", l))
                run(phase("down", l))
                dve.wait_ge(bank_free, tiles_out(phase("down", l)))
                dve.sem_inc(x_done, 1)
            norm(2 * DEPTH)

        @block.gpsimd
        def _(pool):
            own = Chain(pool, pool_own)

            def load_ada(x):
                def one(i, n):
                    c = x.first_chunk + n // KT
                    if not (isinstance(i, int) and x.b0 + i * x.b_per + n < ASLOTS):
                        pool.wait_ge(ada_used, i * x.a_per + (x.a0 + n - ASLOTS + 1))
                    k = n % KT
                    pool.dma_start(ada_raw[:, n % ASLOTS, :],
                                   w_ada[k * P:(k + 1) * P, bass.ds(i * (512 * x.chunks) + c * 512, 512)])\
                        .then_inc(ada_full[n % ASLOTS], 16)

                def body(i):
                    for n in range(x.b_per):
                        one(i, n)
                if x.b_per:
                    body(0)
                    repeat(pool, 1, x.iters, body)

            def loads(l, *names):
                for name in names:
                    load_ada(phase(name, l))

            for l in range(DEPTH):
                if l:
                    pool.wait_ge(x_done, 2 * l)
                own(pool.memset(Lb[:], 0.0))
                own(pool.memset(Rall[:], 0.0))
                pool.memset(Lb[0:FOX, :], 1.0)
                pool.memset(Rall[32:32 + FOX, :], 1.0).then_inc(zero_ready, 1)
                loads(l, "nsaa", "nsab", "foxa", "foxb", "outn", "outf", "up", "down")


_OUT = (P, KT, T)


def kernel(**inputs):
    import numpy as _np
    import concourse.bacc as _bacc
    from concourse import mybir as _mybir
    from concourse.bass_utils import run_bass_kernel_spmd as _run

    g = {k: _np.asarray(v) for k, v in inputs.items()}

    def cols(a, *tail):
        a = a.reshape((a.shape[0], -1, P) + tail)
        return _np.moveaxis(a, 2, 0)

    def per_layer(a):
        return a.reshape(P, DEPTH, -1)

    par = _np.concatenate([
        per_layer(cols(g["attn_norm_g"])),
        per_layer(cols(g["ffn_norm_g"])),
        per_layer(cols(_np.ascontiguousarray(_np.moveaxis(g["conv_w"], 1, 2)), 3)),
        per_layer(cols(g["conv_b"])),
        _np.broadcast_to(g["b_fgate"][None], (P, DEPTH, FOX)),
    ], axis=2).reshape(P, -1)
    par = _np.concatenate([par, g["final_norm_g"].reshape(KT, P).T, g["c"].reshape(KT, P).T,
                           g["b_ada"].reshape(-1, P).T], axis=1)
    pos = _np.stack([g["cmp_pos_k"], g["cmp_pos_v"]], axis=1).transpose(0, 3, 1, 2)
    arrays = {
        "xT": g["x"][0].T.reshape(KT, P, T).transpose(1, 0, 2),
        "par": par,
        "pos": pos,
        "consts": constants(),
    }
    for name in ("w_ada", "w_in", "w_cmp1_k", "w_cmp1_v", "w_cmp2_k", "w_cmp2_v", "w_out", "w_up", "w_down"):
        arrays[name] = g[name]
    arrays["w_ada"] = g["w_ada"].transpose(1, 0, 2).reshape(D, -1)
    arrays = {f"in_{k}": _np.ascontiguousarray(v) for k, v in arrays.items()}
    nc = _bacc.Bacc("TRN2", target_bir_lowering=False, num_devices=1)
    args = [nc.dram_tensor(k, v.shape, _mybir.dt.from_np(v.dtype), kind="ExternalInput").ap()
            for k, v in arrays.items()]
    args.append(nc.dram_tensor("out_T", _OUT, _mybir.dt.float32, kind="ExternalOutput").ap())
    trunk(nc, *args)
    r = _run(nc, [arrays], core_ids=[0])
    got = r.results[0]["out_T"]
    return _np.ascontiguousarray(got.transpose(2, 1, 0).reshape(1, T, D))
```
